# Optimizing a Trainium2 kernel written in Bass

```python
import math
import jax, jax.numpy as jnp
from jax import lax
import numpy as np

D_MODEL = 1024
BATCH = 1
SEQ = 256
DEPTH = 1
DEC_BATCH = 1
DEC_SEQ = 1024
PAST_LEN = 128

MIX_WIDTH = D_MODEL
ATTN_WIDTH = MIX_WIDTH // 2
FOURIER_WIDTH = MIX_WIDTH - ATTN_WIDTH
N_ATTN_HEADS = 4
ATTN_HEAD_V = ATTN_WIDTH // N_ATTN_HEADS
ATTN_HEAD_QK = ATTN_HEAD_V // 2
N_FOURIER_GROUPS = 4
FOURIER_GROUP = FOURIER_WIDTH // N_FOURIER_GROUPS
IN_PROJ_WIDTH = 3 * ATTN_WIDTH + FOURIER_WIDTH
Q_BLOCK = 128
PEER_HEADS = 8
PEER_N_KEYS = 128
PEER_N_EXPERTS = PEER_N_KEYS * PEER_N_KEYS
PEER_QUERY_DIM = 128
PEER_HALF = PEER_QUERY_DIM // 2
PEER_TOPK = 16
TOKEN_BLOCK = 128
LN_EPS = 1e-5
RMS_EPS = 1e-5
DEEPNORM_ALPHA = (2 * DEPTH) ** 0.25
DEEPNORM_BETA = (8 * DEPTH) ** -0.25

kernel_name = 'hybrid_diffattn_fnet_peer_encoder'

def layer_norm(x, g, b):
    xf = x.astype(jnp.float32)
    mu = jnp.mean(xf, axis=-1, keepdims=True)
    xc = xf - mu
    var = jnp.mean(xc * xc, axis=-1, keepdims=True)
    y = xc * lax.rsqrt(var + LN_EPS) * g.astype(jnp.float32) + b.astype(jnp.float32)
    return y.astype(x.dtype)

def alibi_slopes():
    h = jnp.arange(1, N_ATTN_HEADS + 1, dtype=jnp.float32)
    return jnp.exp2(-8.0 * h / N_ATTN_HEADS)

def lambda_init_fn(layer):
    return 0.8 - 0.6 * math.exp(-0.3 * layer)

def diff_attention(q, k, v, lam, slopes):
    B, S = q.shape[0], q.shape[1]
    nb = S // Q_BLOCK
    scale = ATTN_HEAD_QK ** -0.5
    qf = (q.astype(jnp.float32) * scale).reshape(B, nb, Q_BLOCK, N_ATTN_HEADS, 2, ATTN_HEAD_QK)
    qf = qf.transpose(1, 0, 2, 3, 4, 5)
    kf = k.astype(jnp.float32)
    kpos = jnp.arange(S, dtype=jnp.float32)
    starts = jnp.arange(nb, dtype=jnp.int32) * Q_BLOCK

    def block(args):
        qb, start = args
        s = jnp.einsum('bqhcd,bkhcd->bhcqk', qb, kf)
        qpos = (start + jnp.arange(Q_BLOCK, dtype=jnp.int32)).astype(jnp.float32)
        dist = jnp.abs(qpos[:, None] - kpos[None, :])
        s = s - (slopes[:, None, None] * dist)[None, :, None]
        p = jax.nn.softmax(s, axis=-1)
        a = p[:, :, 0] - lam * p[:, :, 1]
        return jnp.einsum('bhqk,bkhe->bqhe', a.astype(v.dtype), v)

    o = lax.map(block, (qf, starts))
    return o.transpose(1, 0, 2, 3, 4).reshape(B, S, N_ATTN_HEADS, ATTN_HEAD_V)

def head_rms_norm(o, g, out_scale):
    of = o.astype(jnp.float32)
    y = of * lax.rsqrt(jnp.mean(of * of, axis=-1, keepdims=True) + RMS_EPS) * g.astype(jnp.float32)
    return (y * out_scale).astype(o.dtype)

def fourier_mix(xf, w_f, b_f):
    z = jnp.fft.fft2(xf.astype(jnp.float32), axes=(1, 3), norm='ortho').real.astype(xf.dtype)
    return jnp.einsum('bsgc,gce->bsge', z, w_f) + b_f

def peer(x, wq, subkeys, u, v):
    B, S, D = x.shape
    xt = x.reshape(-1, TOKEN_BLOCK, D)

    def chunk(xc):
        q = (xc @ wq).reshape(TOKEN_BLOCK, PEER_HEADS, 2, PEER_HALF)
        sc = jnp.einsum('thcd,hcnd->thcn', q.astype(jnp.float32), subkeys.astype(jnp.float32))
        s_top, i_top = lax.top_k(sc, PEER_TOPK)
        cand = s_top[:, :, 0, :, None] + s_top[:, :, 1, None, :]
        cidx = i_top[:, :, 0, :, None] * PEER_N_KEYS + i_top[:, :, 1, None, :]
        cand = cand.reshape(TOKEN_BLOCK, PEER_HEADS, PEER_TOPK * PEER_TOPK)
        cidx = cidx.reshape(TOKEN_BLOCK, PEER_HEADS, PEER_TOPK * PEER_TOPK)
        best, pos = lax.top_k(cand, PEER_TOPK)
        eidx = jnp.take_along_axis(cidx, pos, axis=-1)
        g = jax.nn.softmax(best, axis=-1)
        act = jax.nn.gelu(jnp.einsum('td,thkd->thk', xc, u[eidx]).astype(jnp.float32))
        coef = (g * act).astype(xc.dtype)
        return jnp.einsum('thk,thkd->td', coef, v[eidx])

    return lax.map(chunk, xt).reshape(B, S, D)

def encoder_layer(x, layer, w_in, lq1, lk1, lq2, lk2, subln_g, w_fourier, b_fourier, w_out,
                  ln1_g, ln1_b, peer_wq, peer_subkeys, peer_u, peer_v, ln2_g, ln2_b):
    B, S, _ = x.shape
    h = x @ w_in
    q = h[..., :ATTN_WIDTH].reshape(B, S, N_ATTN_HEADS, 2, ATTN_HEAD_QK)
    k = h[..., ATTN_WIDTH:2 * ATTN_WIDTH].reshape(B, S, N_ATTN_HEADS, 2, ATTN_HEAD_QK)
    v = h[..., 2 * ATTN_WIDTH:3 * ATTN_WIDTH].reshape(B, S, N_ATTN_HEADS, ATTN_HEAD_V)
    xf = h[..., 3 * ATTN_WIDTH:].reshape(B, S, N_FOURIER_GROUPS, FOURIER_GROUP)
    linit = lambda_init_fn(layer)
    lam = (jnp.exp(jnp.sum(lq1.astype(jnp.float32) * lk1.astype(jnp.float32)))
           - jnp.exp(jnp.sum(lq2.astype(jnp.float32) * lk2.astype(jnp.float32))) + linit)
    o = diff_attention(q, k, v, lam, alibi_slopes())
    o = head_rms_norm(o, subln_g, 1.0 - linit).reshape(B, S, ATTN_WIDTH)
    f = fourier_mix(xf, w_fourier, b_fourier).reshape(B, S, FOURIER_WIDTH)
    mix = jnp.concatenate([o, f], axis=-1) @ w_out
    x = layer_norm(DEEPNORM_ALPHA * x + mix, ln1_g, ln1_b)
    x = layer_norm(DEEPNORM_ALPHA * x + peer(x, peer_wq, peer_subkeys, peer_u, peer_v), ln2_g, ln2_b)
    return x

def run_trunk(x, ln_in_g, ln_in_b, w_in, lambda_q1, lambda_k1, lambda_q2, lambda_k2, subln_g,
              w_fourier, b_fourier, w_out, ln1_g, ln1_b, peer_wq, peer_subkeys, peer_u, peer_v,
              ln2_g, ln2_b):
    x = layer_norm(x, ln_in_g, ln_in_b)
    for l in range(DEPTH):
        x = encoder_layer(x, l, w_in[l], lambda_q1[l], lambda_k1[l], lambda_q2[l], lambda_k2[l],
                          subln_g[l], w_fourier[l], b_fourier[l], w_out[l], ln1_g[l], ln1_b[l],
                          peer_wq[l], peer_subkeys[l], peer_u[l], peer_v[l], ln2_g[l], ln2_b[l])
    return x

def setup_inputs(seed: int = 0) -> dict:
    key = jax.random.key(seed)
    ks = jax.random.split(key, 24)
    f32 = jnp.float32

    def nrm(k, shape, scale):
        return jax.random.normal(k, shape, f32) * scale

    col_scale = jnp.concatenate([jnp.ones((2 * ATTN_WIDTH,), f32),
                                 jnp.full((ATTN_WIDTH + FOURIER_WIDTH,), DEEPNORM_BETA, f32)])
    return {
        'x_prompt': nrm(ks[0], (BATCH, SEQ, D_MODEL), 1.0),
        'x_sample': nrm(ks[1], (DEC_BATCH, DEC_SEQ, D_MODEL), 1.0),
        'ln_in_g': 1.0 + nrm(ks[2], (D_MODEL,), 0.02),
        'ln_in_b': nrm(ks[3], (D_MODEL,), 0.02),
        'w_in': nrm(ks[4], (DEPTH, D_MODEL, IN_PROJ_WIDTH), D_MODEL ** -0.5) * col_scale,
        'lambda_q1': nrm(ks[5], (DEPTH, ATTN_HEAD_QK), 0.1),
        'lambda_k1': nrm(ks[6], (DEPTH, ATTN_HEAD_QK), 0.1),
        'lambda_q2': nrm(ks[7], (DEPTH, ATTN_HEAD_QK), 0.1),
        'lambda_k2': nrm(ks[8], (DEPTH, ATTN_HEAD_QK), 0.1),
        'subln_g': 1.0 + nrm(ks[9], (DEPTH, ATTN_HEAD_V), 0.02),
        'w_fourier': nrm(ks[10], (DEPTH, N_FOURIER_GROUPS, FOURIER_GROUP, FOURIER_GROUP),
                         FOURIER_GROUP ** -0.5 * DEEPNORM_BETA),
        'b_fourier': nrm(ks[11], (DEPTH, N_FOURIER_GROUPS, FOURIER_GROUP), 0.02),
        'w_out': nrm(ks[12], (DEPTH, MIX_WIDTH, D_MODEL), MIX_WIDTH ** -0.5 * DEEPNORM_BETA),
        'ln1_g': 1.0 + nrm(ks[13], (DEPTH, D_MODEL), 0.02),
        'ln1_b': nrm(ks[14], (DEPTH, D_MODEL), 0.02),
        'peer_wq': nrm(ks[15], (DEPTH, D_MODEL, PEER_HEADS * PEER_QUERY_DIM), D_MODEL ** -0.5),
        'peer_subkeys': nrm(ks[16], (DEPTH, PEER_HEADS, 2, PEER_N_KEYS, PEER_HALF), PEER_HALF ** -0.5),
        'peer_u': nrm(ks[17], (DEPTH, PEER_N_EXPERTS, D_MODEL), D_MODEL ** -0.5),
        'peer_v': nrm(ks[18], (DEPTH, PEER_N_EXPERTS, D_MODEL), DEEPNORM_BETA),
        'ln2_g': 1.0 + nrm(ks[19], (DEPTH, D_MODEL), 0.02),
        'ln2_b': nrm(ks[20], (DEPTH, D_MODEL), 0.02),
    }

def reference(x_prompt, x_sample, ln_in_g, ln_in_b, w_in, lambda_q1, lambda_k1, lambda_q2,
              lambda_k2, subln_g, w_fourier, b_fourier, w_out, ln1_g, ln1_b, peer_wq,
              peer_subkeys, peer_u, peer_v, ln2_g, ln2_b):
    y_prompt = run_trunk(x_prompt, ln_in_g, ln_in_b, w_in, lambda_q1, lambda_k1, lambda_q2,
                         lambda_k2, subln_g, w_fourier, b_fourier, w_out, ln1_g, ln1_b, peer_wq,
                         peer_subkeys, peer_u, peer_v, ln2_g, ln2_b)
    y_sample = run_trunk(x_sample, ln_in_g, ln_in_b, w_in, lambda_q1, lambda_k1, lambda_q2,
                         lambda_k2, subln_g, w_fourier, b_fourier, w_out, ln1_g, ln1_b, peer_wq,
                         peer_subkeys, peer_u, peer_v, ln2_g, ln2_b)
    return (y_prompt, y_sample)


_drawn_inputs = setup_inputs


def setup_inputs(seed=0):
    import zlib

    import numpy as np

    out = dict(_drawn_inputs(seed))
    spreads = {}
    factors = {}
    for name, (base, spread) in spreads.items():
        noise = np.random.default_rng([zlib.crc32(name.encode()), seed]).standard_normal(out[name].shape)
        drawn = base * np.exp(spread * noise) if base else spread * noise
        out[name] = __import__('jax').numpy.asarray(drawn.astype(out[name].dtype))
    for name, factor in factors.items():
        out[name] = (out[name] * factor).astype(out[name].dtype)
    return out
```

```python
from contextlib import ExitStack

import numpy as np

import concourse.bass as bass
from concourse import mybir

F32 = mybir.dt.float32
U32 = mybir.dt.uint32
ALU = mybir.AluOpType
ACT = mybir.ActivationFunctionType
AX = mybir.AxisListType

P = 128
D = 1024
DC = D // P
S_PROMPT, S_SAMPLE = 256, 1024
NT = (S_PROMPT + S_SAMPLE) // P
T = NT * P
H = 4
HF = 4
DQK = 64
PH = 8
NK = 128
TOPK = 16
NSLOT = PH * TOPK
EPS = 1e-5
ALPHA = 2.0 ** 0.25
LAMBDA_INIT = 0.8 - 0.6
OUT_SCALE = 1.0 - LAMBDA_INIT
SLOPES = [2.0 ** (-8.0 * (h + 1) / H) for h in range(H)]
BATCHES = [(2, S_SAMPLE // P), (0, S_PROMPT // P)]
DIST_W = 2 * S_SAMPLE - P
RING = 8
GELU_A = 0.044715
GELU_B = 2.0 * (2.0 / np.pi) ** 0.5
V_ON_DVE = 4
NEG = -3.0e38


def token_blocks():
    return [(a, min(a + 512, T)) for a in range(0, T, 512)]


def build(nc, x, ln_g, ln_b, w_in, lq1, lk1, lq2, lk2, subln_g, w_f, b_f, w_out, ln1_g, ln1_b,
          wq, skt, pu, pv, ln2_g, ln2_b, dft_sample, dft_prompt, dft_chan, out):
    ctx = ExitStack()
    with ctx:
        def sb(name, cols, dt=F32):
            return ctx.enter_context(nc.sbuf_tensor(name, [P, cols], dt))

        def sem(name):
            return ctx.enter_context(nc.semaphore(name))

        big = sb("big", NT * 2 * D)
        xln = sb("xln", NT * D)
        qk = sb("qk", DC * T)
        wbuf = sb("wbuf", 8 * D)
        gb = sb("gb", 2 * D)
        ident = sb("ident", P)
        small = sb("small", 1500)
        idx_sb = sb("idx_sb", 2 * NSLOT, U32)

        xt = big[:, 0:DC * T].rearrange("p (c t) -> p c t", c=DC)
        vf = big[:, DC * T:].rearrange("p (t n) -> p t n", t=NT)
        sc = big[:, :].rearrange("p (t r) -> p t r", t=NT)
        xn = xln[:, :].rearrange("p (t n) -> p t n", t=NT)
        qkv = qk[:, :].rearrange("p (c t) -> p c t", c=DC)
        w8 = wbuf[:, :].rearrange("p (m c n) -> p m c n", m=8, c=DC)
        w2 = wbuf[:, :].rearrange("p (m c n) -> p m c n", m=2, c=DC)
        wfull = wbuf[:, :].rearrange("p (c n) -> p c n", c=DC)
        g_row, b_row = gb[:, 0:D], gb[:, D:2 * D]
        cc, scn = gb[:, 0:P], gb[:, P:2 * P]
        wf = gb[:, 2 * P:2 * P + HF * P].rearrange("p (g e) -> p g e", g=HF)
        bf = gb[:, 6 * P:6 * P + HF]
        trig = big[:, 0:4096].rearrange("p (k g s) -> p k g s", k=2, g=HF)
        zt = big[:, 4096:5120].rearrange("p (b s) -> p b s", b=2)
        dist = wbuf[:, 0:DIST_W]
        bias_h = wbuf[:, DIST_W:2 * DIST_W]
        o0 = 2 * DIST_W
        prob = wbuf[:, o0:o0 + 2 * D].rearrange("p (c k) -> p c k", c=2)
        diff = wbuf[:, o0 + 2 * D:o0 + 3 * D]
        difft = wbuf[:, o0 + 3 * D:o0 + 4 * D].rearrange("p (k q) -> p k q", k=8)
        assert o0 + 4 * D <= 8 * D
        sk = gb[:, 0:PH * NK].rearrange("p (h n) -> p h n", h=PH)

        n_small = [0]

        def sm(cols):
            a = n_small[0]
            n_small[0] += cols
            assert n_small[0] <= 1500
            return small[:, a:a + cols]

        stats = sm(NT * 12).rearrange("p (t s) -> p t s", t=NT)
        mv = sm(NT * 2).rearrange("p (t s) -> p t s", t=NT)
        veps = sm(NT)
        std = sm(NT)
        rstd = sm(NT)
        diags = sm(4 * P).rearrange("p (b n) -> p b n", b=4)
        n_mark = n_small[0]
        lam4 = sm(4 * DQK).rearrange("p (a d) -> p a d", a=4)
        sub_g = sm(P)
        lam2, elam, nlam = sm(2), sm(2), sm(1)
        rmax = sm(2)
        nrmax = sm(2)
        psum_row = sm(2)
        rinv = sm(2)
        ssq = sm(NT * H)
        rms = sm(NT * H)
        rrms = sm(NT * H)
        n_small[0] = n_mark
        iota16 = sm(TOPK)
        mx8 = sm(PH)
        act = sm(NSLOT)
        coef = sm(NSLOT)
        gate = sm(NSLOT)
        best = sm(NSLOT).rearrange("p (h k) -> p h k", h=PH)
        gsum = sm(PH)
        lnrow = sm(12 + 2 + 3)

        at = [0]

        def wk(cols):
            a = at[0]
            at[0] += cols
            assert at[0] <= DC * T
            return qk[:, a:a + cols]

        scur = wk(2 * PH * NK).rearrange("p (r n) -> p r n", r=2 * PH)
        cand = wk(PH * TOPK * TOPK)
        pick = wk(NSLOT * TOPK)
        xcur = wk(D)
        acc = wk(D)
        vals = wk(2 * PH * TOPK).rearrange("p (r k) -> p r k", r=2 * PH)
        idf = wk(2 * PH * TOPK)
        pabf = wk(2 * NSLOT).rearrange("p (c s) -> p c s", c=2)
        iab = wk(2 * NSLOT).rearrange("p (c s) -> p c s", c=2)
        eidf = wk(NSLOT)
        gt = [wk(NSLOT) for _ in range(3)]
        idx = idx_sb[:, :].rearrange("p (b s) -> p b s", b=2)
        posu = wk(NSLOT).bitcast(U32).rearrange("p (h k) -> p h k", h=PH)
        pshift = wk(NSLOT).bitcast(U32)
        iu = wk(2 * PH * TOPK).bitcast(U32).rearrange("p (r k) -> p r k", r=2 * PH)
        ring = wbuf[:, :].rearrange("p (b n) -> p b n", b=RING)

        banks = [ctx.enter_context(nc.psum_tensor(f"bank{b}", [P, 512], F32)) for b in range(4)]
        wide = [ctx.enter_context(nc.psum_tensor(f"wide{b}", [P, 1024], F32)) for b in range(2)]

        def bank(n):
            return banks[n][:, :] if n < 4 else wide[(n - 4) // 2][:, 512 * (n % 2):512 * (n % 2) + 512]

        x_in = [sem(f"x_in{t}") for t in range(NT)]
        gain_in = [sem(f"gain_in{k}") for k in range(3)]
        w_qk_in = [sem(f"w_qk_in{m}") for m in range(8)]
        w_vf_in = [sem(f"w_vf_in{m}") for m in range(2)]
        dft_in = [sem(f"dft_in{k}") for k in range(2)]
        four_in = sem("four_in")
        lam_in = sem("lam_in")
        w_out_in = sem("w_out_in")
        wq_in = [sem(f"wq_in{m}") for m in range(8)]
        sk_in = sem("sk_in")
        const_done = sem("const_done")
        dve_chain = sem("dve_chain")
        var_done = sem("var_done")
        std_done = sem("std_done")
        ln_in_done = sem("ln_in_done")
        xt_mm, xt_ev = sem("xt_mm"), sem("xt_ev")
        qk_mm, qk_ev = sem("qk_mm"), sem("qk_ev")
        vf_mm, vf_ev = sem("vf_mm"), sem("vf_ev")
        dft_mm, dft_ev = sem("dft_mm"), sem("dft_ev")
        z_mm, z_ev = sem("z_mm"), sem("z_ev")
        f_mm, f_ev = sem("f_mm"), sem("f_ev")
        lam_dots, lam_exp = sem("lam_dots"), sem("lam_exp")
        s_mm, biased, exped, diffed = sem("s_mm"), sem("biased"), sem("exped"), sem("diffed")
        at_mm, at_ev, pv_mm, o_ev = sem("at_mm"), sem("at_ev"), sem("pv_mm"), sem("o_ev")
        ssq_done, rms_done, o_norm = sem("ssq_done"), sem("rms_done"), sem("o_norm")
        ot_mm, ot_ev = sem("ot_mm"), sem("ot_ev")
        wo_mm, wo_add = sem("wo_mm"), sem("wo_add")
        x1_done = sem("x1_done")
        x1t_mm, x1t_ev = sem("x1t_mm"), sem("x1t_ev")
        wq_mm, wq_ev = sem("wq_mm"), sem("wq_ev")
        sc_mm, sc_ev = sem("sc_mm"), sem("sc_ev")
        iota_done = sem("iota_done")
        sc_cur, x_cur = sem("sc_cur"), sem("x_cur")
        chain = sem("chain")
        sc_used, best_sub, gate_exp = sem("sc_used"), sem("best_sub"), sem("gate_exp")
        idx_ready = sem("idx_ready")
        gelu_arg, gelu_exp = sem("gelu_arg"), sem("gelu_exp")
        acc_init = sem("acc_init")
        dot_done = sem("dot_done")
        diag_ready = sem("diag_ready")
        v_mm = sem("v_mm")
        var2, std2 = sem("var2"), sem("std2")
        y_ready, y_out, y_stored = sem("y_ready"), sem("y_out"), sem("y_stored")
        y_taken = sem("y_taken")
        slots_free, scores_seen = sem("slots_free"), sem("scores_seen")
        row_in = [sem(f"row_in{k}") for k in range(RING)]
        row_used = [sem(f"row_used{k}") for k in range(RING)]

        block = ctx.enter_context(nc.Block())

        V_PE = [s for s in range(NSLOT) if s % V_ON_DVE != V_ON_DVE - 1]
        USES = 2 * NSLOT // RING

        def use(t, s, v):
            return t * USES + (v * NSLOT + s) // RING + 1

        @block.sync
        def _(sp):
            for t in range(NT):
                sp.dma_start(xn[:, t, :], x[t * P:(t + 1) * P, :]).then_inc(x_in[t], 16)
                if t == 1:
                    sp.dma_start(g_row, ln_g.partition_broadcast(P)).then_inc(gain_in[0], 16)
                    sp.dma_start(b_row, ln_b.partition_broadcast(P)).then_inc(gain_in[0], 16)
            w_in_v = w_in.rearrange("(c p) n -> p c n", p=P)
            for m in range(8):
                sp.dma_start(w8[:, m], w_in_v[:, :, m * P:(m + 1) * P]).then_inc(w_qk_in[m], 16)
            for a, v in enumerate((lq1, lk1, lq2, lk2)):
                sp.dma_start(lam4[:, a, :], v.partition_broadcast(P)).then_inc(lam_in, 16)
            sp.dma_start(sub_g, subln_g.partition_broadcast(P)).then_inc(lam_in, 16)
            blocks = len(token_blocks())
            for m in range(2):
                sp.wait_ge(qk_mm, 4 * (m + 1) * blocks)
                sp.dma_start(w2[:, m], w_in_v[:, :, D + 512 * m:D + 512 * (m + 1)]).then_inc(w_vf_in[m], 16)
            sp.wait_ge(ln_in_done, NT)
            sp.dma_start(cc, dft_chan[0]).then_inc(four_in, 16)
            sp.dma_start(scn, dft_chan[1]).then_inc(four_in, 16)
            sp.dma_start(wf, w_f.rearrange("g c e -> c g e")).then_inc(four_in, 16)
            sp.dma_start(bf, b_f.rearrange("g e -> e g"), allow_slow_non_contiguous=True).then_inc(four_in, 16)
            for n in range(3):
                for k in range(2):
                    if n == 0:
                        sp.wait_ge(vf_mm, NT * (k + 1))
                    else:
                        sp.wait_ge(dft_mm, 2 * HF * (n - 1) + HF * (k + 1))
                    if n < 2:
                        sp.dma_start(w2[:, k], dft_sample[k].rearrange("(c p) s -> p c s", p=P)[
                            :, :, 512 * n:512 * n + 512]).then_inc(dft_in[k], 16)
                    else:
                        sp.dma_start(w2[:, k, 0:2, 0:S_PROMPT],
                                     dft_prompt[k].rearrange("(c p) s -> p c s", p=P)).then_inc(dft_in[k], 16)
            sp.wait_ge(f_mm, 3 * HF)
            sp.wait_ge(f_ev, 3 * HF)
            sp.dma_start(g_row, ln1_g.partition_broadcast(P)).then_inc(gain_in[1], 16)
            sp.dma_start(b_row, ln1_b.partition_broadcast(P)).then_inc(gain_in[1], 16)
            sp.wait_ge(pv_mm, NT * H)
            sp.wait_ge(diffed, NT * H)
            sp.dma_start(wfull, w_out.rearrange("(c p) n -> p c n", p=P)).then_inc(w_out_in, 16)
            sp.wait_ge(wo_mm, 2 * NT)
            wq_v = wq.rearrange("(c p) n -> p c n", p=P)
            for m in range(8):
                sp.dma_start(w8[:, m], wq_v[:, :, m * P:(m + 1) * P]).then_inc(wq_in[m], 16)
            sp.wait_ge(x1_done, NT)
            sp.dma_start(sk, skt.rearrange("c d h n -> (c d) h n")).then_inc(sk_in, 16)
            sp.wait_ge(sc_mm, 4 * NT)
            sp.dma_start(g_row, ln2_g.partition_broadcast(P)).then_inc(gain_in[2], 16)
            sp.dma_start(b_row, ln2_b.partition_broadcast(P)).then_inc(gain_in[2], 16)
            sp.sem_inc(y_stored, 1)
            with sp.Fori(0, NT) as t:
                sp.wait_ge(y_ready, t + 1)
                sp.dma_start(out[bass.ds(t * P, P), :], acc).then_inc(y_out, 16)
                sp.wait_ge(y_out, t * 16 + 16)
                sp.sem_inc(y_stored, 1)

        @block.gpsimd
        def _(pool):
            pool.memset(ident[:, :], 0.0).then_inc(const_done, 1)
            pool.wait_ge(const_done, 1)
            pool.affine_select(out=ident[:, :], in_=ident[:, :], compare_op=ALU.not_equal, fill=1.0, base=0,
                               pattern=[[-1, P]], channel_multiplier=1).then_inc(const_done, 1)
            pool.wait_ge(dft_mm, 3 * 2 * HF)
            pool.iota(dist, pattern=[[-1, DIST_W]], base=S_SAMPLE - P, channel_multiplier=1,
                      allow_small_or_imprecise_dtypes=True).then_inc(iota_done, 1)
            pool.wait_ge(o_norm, NT)
            pool.wait_ge(ot_ev, NT)
            pool.iota(iota16, pattern=[[1, TOPK]], base=0, channel_multiplier=0,
                      allow_small_or_imprecise_dtypes=True).then_inc(iota_done, 1)
            pool.wait_ge(wq_mm, 8 * len(token_blocks()))

            def gathers(t, par):
                pool.wait_ge(idx_ready, t + 1)
                for v, table in enumerate((pu, pv)):
                    for s in range(NSLOT):
                        k = s % RING
                        pool.wait_ge(row_used[k], use(t, s, v))
                        pool.sem_inc(slots_free, 1)
                        pool.indirect_dma_start(
                            ring[:, k, :], None, table,
                            bass.IndirectOffsetOnAxis(ap=idx[:, par, s:s + 1], axis=0)).then_inc(row_in[k], 16)

            for k in range(RING):
                pool.sem_inc(row_used[k], 1)
            with pool.Fori(0, NT // 2) as i:
                for par in range(2):
                    gathers(i * 2 + par, par)

        def att_groups(u, k):
            per_head = sum(nt * ((nt + 3) // 4) for _, nt in BATCHES)
            h, r = divmod(u, NT)
            n = h * per_head
            for _, nt in BATCHES:
                g = (nt + 3) // 4
                if r < nt:
                    return n + r * g + k // 4
                n += nt * g
                r -= nt

        @block.scalar
        def _(act_e):
            def evac(dst, src, func=ACT.Copy, **kw):
                return nc.scalar.activation(dst, src, func, **kw)

            act_e.wait_ge(var_done, 1)
            nc.scalar.activation(std, veps, ACT.Sqrt).then_inc(std_done, 1)
            for n in range(2 * NT):
                t, half = divmod(n, 2)
                act_e.wait_ge(xt_mm, n + 1)
                evac(xt[:, 4 * half:4 * half + 4, t * P:(t + 1) * P],
                     bank(n % 8).rearrange("p (c t) -> p c t", c=4)).then_inc(xt_ev, 1)
            n = 0
            for m in range(8):
                for a, b in token_blocks():
                    act_e.wait_ge(qk_mm, n + 1)
                    evac(qkv[:, m, a:b], bank(n % 8)[:, 0:b - a], scale=DQK ** -0.5 if m < 4 else 1.0)\
                        .then_inc(qk_ev, 1)
                    n += 1
            n = 0
            for m in range(2):
                for t in range(NT):
                    act_e.wait_ge(vf_mm, n + 1)
                    evac(vf[:, t, 512 * m:512 * m + 512], bank(n % 8)).then_inc(vf_ev, 1)
                    n += 1
            act_e.wait_ge(lam_dots, 1)
            nc.scalar.activation(elam, lam2, ACT.Exp).then_inc(lam_exp, 1)
            act_e.wait_ge(four_in, 64)
            for n in range(3):
                w = 512 if n < 2 else S_PROMPT
                tok = S_PROMPT + 512 * n if n < 2 else 0
                for j in range(2 * HF):
                    act_e.wait_ge(dft_mm, 2 * HF * n + j + 1)
                    if n > 0:
                        act_e.wait_ge(z_mm, HF * n)
                    evac(trig[:, j // HF, j % HF, 0:w], bank(j % 4)[:, 0:w]).then_inc(dft_ev, 1)
                for g in range(HF):
                    m = HF * n + g
                    act_e.wait_ge(z_mm, m + 1)
                    if m >= 2:
                        act_e.wait_ge(f_mm, m - 1)
                    evac(zt[:, m % 2, 0:w], bank(4 + m % 2)[:, 0:w]).then_inc(z_ev, 1)
                    act_e.wait_ge(f_mm, m + 1)
                    nc.scalar.activation(xt[:, 4 + g, tok:tok + w], bank(6 + m % 2)[:, 0:w], ACT.Identity,
                                         bias=bf[:, g:g + 1]).then_inc(f_ev, 1)
            u = 0
            for h in range(H):
                for t0, nt in BATCHES:
                    for qt in range(nt):
                        for c in range(2):
                            act_e.wait_ge(biased, 2 * u + c + 1)
                            keys = prob[:, c, 0:nt * P]
                            nc.scalar.activation(keys, keys, ACT.Exp, bias=nrmax[:, c:c + 1],
                                                 accum_out=psum_row[:, c:c + 1]).then_inc(exped, 1)
                        for k in range(0, nt, 4):
                            n = min(4, nt - k)
                            act_e.wait_ge(at_mm, att_groups(u, k) + 1)
                            if u:
                                act_e.wait_ge(pv_mm, u)
                            evac(difft[:, k:k + n, :], bank(k // 4)[:, 0:n * P].rearrange("p (k q) -> p k q", q=P))\
                                .then_inc(at_ev, 1)
                        u += 1
            act_e.wait_ge(ssq_done, 1)
            nc.scalar.activation(rms, ssq, ACT.Sqrt).then_inc(rms_done, 1)
            for t in range(NT):
                act_e.wait_ge(ot_mm, t + 1)
                evac(xt[:, 0:4, t * P:(t + 1) * P], bank(t % 8).rearrange("p (c t) -> p c t", c=4))\
                    .then_inc(ot_ev, 1)
            act_e.wait_ge(var_done, 2)
            nc.scalar.activation(std, veps, ACT.Sqrt).then_inc(std_done, 1)
            act_e.wait_ge(wo_mm, 2 * NT)
            for n in range(2 * NT):
                t, half = divmod(n, 2)
                act_e.wait_ge(x1t_mm, n + 1)
                evac(xt[:, 4 * half:4 * half + 4, t * P:(t + 1) * P],
                     bank(n % 8).rearrange("p (c t) -> p c t", c=4)).then_inc(x1t_ev, 1)
            n = 0
            for m in range(8):
                for a, b in token_blocks():
                    act_e.wait_ge(wq_mm, n + 1)
                    evac(qkv[:, m, a:b], bank(n % 8)[:, 0:b - a]).then_inc(wq_ev, 1)
                    n += 1
            for n in range(4 * NT):
                act_e.wait_ge(sc_mm, n + 1)
                evac(sc[:, n // 4, 512 * (n % 4):512 * (n % 4) + 512], bank(n % 8)).then_inc(sc_ev, 1)

            def load_scores(t, copies):
                if copies is not None:
                    act_e.wait_ge(sc_used, copies)
                evac(scur.rearrange("p r n -> p (r n)"), sc[:, bass.ds(t, 1), :].rearrange("p a r -> p (a r)"))\
                    .then_inc(sc_cur, 1)

            def load_x(t):
                evac(xcur, xn[:, bass.ds(t, 1), :].rearrange("p a r -> p (a r)")).then_inc(x_cur, 1)

            def gate_exps(t):
                act_e.wait_ge(best_sub, t + 1)
                flat = best.rearrange("p h k -> p (h k)")
                nc.scalar.activation(flat, flat, ACT.Exp).then_inc(gate_exp, 1)

            def tile(t, last):
                if not last:
                    load_scores(t + 1, t + 1)
                act_e.wait_ge(gelu_arg, t + 1)
                nc.scalar.activation(gt[1], gt[0], ACT.Exp, scale=-GELU_B).then_inc(gelu_exp, 1)
                if not last:
                    act_e.wait_ge(acc_init, t + 1)
                    load_x(t + 1)
                    gate_exps(t + 1)
                act_e.wait_ge(var2, t + 1)
                nc.scalar.activation(lnrow[:, 15:16], lnrow[:, 14:15], ACT.Sqrt).then_inc(std2, 1)

            act_e.wait_ge(sc_ev, 4 * NT)
            act_e.wait_ge(sc_mm, 4 * NT)
            load_scores(0, None)
            load_x(0)
            gate_exps(0)
            with act_e.Fori(0, NT - 1) as t:
                tile(t, False)
            tile(NT - 1, True)

        @block.tensor
        def _(pe):
            pe.wait_ge(const_done, 2)
            for n in range(2 * NT):
                t, half = divmod(n, 2)
                if half == 0:
                    pe.wait_ge(ln_in_done, t + 1)
                if n >= 8:
                    pe.wait_ge(xt_ev, n - 7)
                for c in range(4):
                    j = 4 * half + c
                    last = nc.tensor.transpose(bank(n % 8)[:, c * P:(c + 1) * P], xn[:, t, j * P:(j + 1) * P],
                                               ident[:, :])
                last.then_inc(xt_mm, 1)
            pe.wait_ge(xt_ev, 2 * NT)
            n = 0
            for m in range(8):
                pe.wait_ge(w_qk_in[m], 16)
                for a, b in token_blocks():
                    if n >= 8:
                        pe.wait_ge(qk_ev, n - 7)
                    for c in range(DC):
                        last = nc.tensor.matmul(bank(n % 8)[:, 0:b - a], w8[:, m, c, :], xt[:, c, a:b],
                                                start=(c == 0), stop=(c == DC - 1))
                    last.then_inc(qk_mm, 1)
                    n += 1
            pe.wait_ge(qk_ev, 8 * len(token_blocks()))
            n = 0
            for m in range(2):
                pe.wait_ge(w_vf_in[m], 16)
                for t in range(NT):
                    if n >= 8:
                        pe.wait_ge(vf_ev, n - 7)
                    for c in range(DC):
                        last = nc.tensor.matmul(bank(n % 8), xt[:, c, t * P:(t + 1) * P], w2[:, m, c, :],
                                                start=(c == 0), stop=(c == DC - 1))
                    last.then_inc(vf_mm, 1)
                    n += 1
            pe.wait_ge(vf_ev, 2 * NT)
            pe.wait_ge(four_in, 64)
            for n in range(3):
                w, t0, nc_k = (512, 2, 8) if n < 2 else (S_PROMPT, 0, 2)
                for j in range(2 * HF):
                    k, g = divmod(j, HF)
                    if g == 0:
                        pe.wait_ge(dft_in[k], 16 * (n + 1))
                    if 2 * HF * n + j >= 4:
                        pe.wait_ge(dft_ev, 2 * HF * n + j - 3)
                    for c in range(nc_k):
                        last = nc.tensor.matmul(bank(j % 4)[:, 0:w], vf[:, t0 + c, 512 + g * P:512 + (g + 1) * P],
                                                w2[:, k, c, 0:w], start=(c == 0), stop=(c == nc_k - 1))
                    last.then_inc(dft_mm, 1)
                for g in range(HF):
                    m = HF * n + g
                    pe.wait_ge(dft_ev, 2 * HF * n + HF + g + 1)
                    if m >= 2:
                        pe.wait_ge(z_ev, m - 1)
                    nc.tensor.matmul(bank(4 + m % 2)[:, 0:w], cc, trig[:, 0, g, 0:w], start=True, stop=False)
                    nc.tensor.matmul(bank(4 + m % 2)[:, 0:w], scn, trig[:, 1, g, 0:w], start=False, stop=True)\
                        .then_inc(z_mm, 1)
                    pe.wait_ge(z_ev, m + 1)
                    if m >= 2:
                        pe.wait_ge(f_ev, m - 1)
                    nc.tensor.matmul(bank(6 + m % 2)[:, 0:w], wf[:, g, :], zt[:, m % 2, 0:w],
                                     start=True, stop=True).then_inc(f_mm, 1)
            pe.wait_ge(f_ev, 3 * HF)

            units = [(h, t0, nt, qt) for h in range(H) for t0, nt in BATCHES for qt in range(nt)]

            def scores(u):
                h, t0, nt, qt = units[u]
                q0, k0 = (t0 + qt) * P, t0 * P
                for c in range(2):
                    if u:
                        pe.wait_ge(biased, 2 * (u - 1) + c + 1)
                    rows = slice(c * DQK, (c + 1) * DQK)
                    for k in range(0, nt * P, 512):
                        w = min(512, nt * P - k)
                        last = nc.tensor.matmul(wide[c][:, k:k + w], qkv[rows, h, q0:q0 + P],
                                                qkv[rows, 4 + h, k0 + k:k0 + k + w], start=True, stop=True)
                    last.then_inc(s_mm, 1)

            def mix_values(u):
                h, t0, nt, qt = units[u]
                pe.wait_ge(diffed, u + 1)
                for k in range(0, nt, 4):
                    if att_groups(u, k) >= 1:
                        pe.wait_ge(at_ev, max(1, att_groups(u, 0)))
                    for j in range(k, min(k + 4, nt)):
                        last = nc.tensor.transpose(bank(k // 4)[:, (j - k) * P:(j - k + 1) * P],
                                                   diff[:, j * P:(j + 1) * P], ident[:, :])
                    last.then_inc(at_mm, 1)
                for j in range(nt):
                    if j % 4 == 0:
                        pe.wait_ge(at_ev, att_groups(u, j) + 1)
                    if u >= 2 and j == 0:
                        pe.wait_ge(o_ev, u - 1)
                    last = nc.tensor.matmul(bank(2 + u % 2)[:, 0:P], difft[:, j, :], vf[:, t0 + j, h * P:(h + 1) * P],
                                            start=(j == 0), stop=(j == nt - 1))
                last.then_inc(pv_mm, 1)

            scores(0)
            for u in range(len(units)):
                if u + 1 < len(units):
                    scores(u + 1)
                mix_values(u)
            for t in range(NT):
                pe.wait_ge(o_norm, t + 1)
                if t >= 8:
                    pe.wait_ge(ot_ev, t - 7)
                for h in range(H):
                    last = nc.tensor.transpose(bank(t % 8)[:, h * P:(h + 1) * P],
                                               vf[:, t, 512 + h * P:512 + (h + 1) * P], ident[:, :])
                last.then_inc(ot_mm, 1)
            pe.wait_ge(w_out_in, 16)
            pe.wait_ge(ot_ev, NT)
            for n in range(2 * NT):
                t, half = divmod(n, 2)
                if n >= 8:
                    pe.wait_ge(wo_add, n - 7)
                for c in range(DC):
                    last = nc.tensor.matmul(bank(n % 8), xt[:, c, t * P:(t + 1) * P],
                                            wfull[:, c, 512 * half:512 * half + 512],
                                            start=(c == 0), stop=(c == DC - 1))
                last.then_inc(wo_mm, 1)
            pe.wait_ge(wo_add, 2 * NT)
            for n in range(2 * NT):
                t, half = divmod(n, 2)
                if half == 0:
                    pe.wait_ge(x1_done, t + 1)
                if n >= 8:
                    pe.wait_ge(x1t_ev, n - 7)
                for c in range(4):
                    j = 4 * half + c
                    last = nc.tensor.transpose(bank(n % 8)[:, c * P:(c + 1) * P], xn[:, t, j * P:(j + 1) * P],
                                               ident[:, :])
                last.then_inc(x1t_mm, 1)
            pe.wait_ge(x1t_ev, 2 * NT)
            n = 0
            for m in range(8):
                pe.wait_ge(wq_in[m], 16)
                for a, b in token_blocks():
                    if n >= 8:
                        pe.wait_ge(wq_ev, n - 7)
                    for c in range(DC):
                        last = nc.tensor.matmul(bank(n % 8)[:, 0:b - a], w8[:, m, c, :], xt[:, c, a:b],
                                                start=(c == 0), stop=(c == DC - 1))
                    last.then_inc(wq_mm, 1)
                    n += 1
            pe.wait_ge(wq_ev, 8 * len(token_blocks()))
            pe.wait_ge(sk_in, 16)
            for n in range(4 * NT):
                t, c, h4 = n // 4, (n % 4) // 2, n % 2
                if n >= 8:
                    pe.wait_ge(sc_ev, n - 7)
                rows = slice(c * DQK, (c + 1) * DQK)
                for j in range(4):
                    h = 4 * h4 + j
                    last = nc.tensor.matmul(bank(n % 8)[:, j * NK:(j + 1) * NK], qkv[rows, h, t * P:(t + 1) * P],
                                            sk[rows, h, :], start=True, stop=True)
                last.then_inc(sc_mm, 1)
            pe.wait_ge(sc_ev, 4 * NT)

            y = wide[0]

            def values(t):
                for n, s in enumerate(V_PE):
                    pe.wait_ge(diag_ready, t * len(V_PE) + n + 1)
                    pe.wait_ge(row_in[s % RING], use(t, s, 1) * 16)
                    for half in range(2):
                        last = nc.tensor.matmul(y[:, 512 * half:512 * half + 512], diags[:, n % 4, :],
                                                ring[:, s % RING, 512 * half:512 * half + 512],
                                                start=(n == 0), stop=(n == len(V_PE) - 1), skip_group_check=True)
                    last.then_inc(row_used[s % RING], 1)

            pe.sem_inc(y_taken, 1)
            with pe.Fori(0, NT) as t:
                pe.wait_ge(y_taken, t + 1)
                values(t)

        @block.vector
        def _(dve):
            done = [0]

            def link(ins):
                done[0] += 1
                ins.then_inc(dve_chain, 1)
                dve.wait_ge(dve_chain, done[0])

            def ln_stats(t):
                for j in range(2):
                    link(nc.vector.bn_stats(stats[:, t, 6 * j:6 * j + 6], xn[:, t, 512 * j:512 * j + 512]))
                link(nc.vector.bn_aggr(mv[:, t, :], stats[:, t, :]))

            def ln_apply(which, ready):
                nc.vector.tensor_scalar(veps, mv[:, :, 1], EPS, None, ALU.add).then_inc(var_done, 1)
                dve.wait_ge(std_done, which + 1)
                link(nc.vector.reciprocal(rstd, std))
                dve.wait_ge(gain_in[which], 32)
                for t in range(NT):
                    r = xn[:, t, :]
                    link(nc.vector.tensor_scalar(r, r, mv[:, t, 0:1], rstd[:, t:t + 1], ALU.subtract, ALU.mult))
                    link(nc.vector.tensor_tensor(r, r, g_row, ALU.mult))
                    nc.vector.tensor_tensor(r, r, b_row, ALU.add).then_inc(ready, 1)

            for t in range(NT):
                dve.wait_ge(x_in[t], 16)
                ln_stats(t)
            ln_apply(0, ln_in_done)
            dve.wait_ge(lam_in, 80)
            for a in range(2):
                link(nc.vector.tensor_tensor_reduce(lam4[:, 2 * a, :], lam4[:, 2 * a, :], lam4[:, 2 * a + 1, :],
                                                    1.0, 0.0, ALU.mult, ALU.add, lam2[:, a:a + 1]))
            nc.vector.tensor_scalar(lam2, lam2, 0.0, None, ALU.add).then_inc(lam_dots, 1)
            dve.wait_ge(lam_exp, 1)
            link(nc.vector.tensor_scalar(nlam, elam[:, 1:2], elam[:, 0:1], -LAMBDA_INIT, ALU.subtract, ALU.add))
            link(nc.vector.tensor_scalar(sub_g, sub_g, OUT_SCALE, None, ALU.mult))

            dve.wait_ge(iota_done, 1)
            link(nc.vector.tensor_scalar(bias_h, dist, -1.0, None, ALU.mult))
            link(nc.vector.tensor_tensor(dist, dist, bias_h, ALU.max))
            u = 0

            def take_output(v, h, tq):
                dve.wait_ge(pv_mm, v + 1)
                o = vf[:, tq, 512 + h * P:512 + (h + 1) * P]
                nc.vector.tensor_copy(o, bank(2 + v % 2)[:, 0:P]).then_inc(o_ev, 1)

            units = [(h, t0, nt, qt) for h in range(H) for t0, nt in BATCHES for qt in range(nt)]
            for u, (h, t0, nt, qt) in enumerate(units):
                if u % NT == 0:
                    link(nc.vector.tensor_scalar(bias_h, dist, -SLOPES[h], None, ALU.mult))
                w = nt * P
                first = S_SAMPLE - P - qt * P
                for c in range(2):
                    dve.wait_ge(s_mm, 2 * u + c + 1)
                    link(nc.vector.tensor_tensor_reduce(prob[:, c, 0:w], wide[c][:, 0:w], bias_h[:, first:first + w],
                                                        1.0, -3.0e38, ALU.add, ALU.max, rmax[:, c:c + 1]))
                    nc.vector.tensor_scalar(nrmax[:, c:c + 1], rmax[:, c:c + 1], -1.0, None, ALU.mult)\
                        .then_inc(biased, 1)
                if u >= 1:
                    hh, tt0, _, qq = units[u - 1]
                    take_output(u - 1, hh, tt0 + qq)
                dve.wait_ge(exped, 2 * u + 2)
                link(nc.vector.reciprocal(rinv, psum_row))
                link(nc.vector.tensor_scalar(rinv[:, 1:2], rinv[:, 1:2], nlam, None, ALU.mult))
                if u:
                    dve.wait_ge(at_mm, att_groups(u, 0))
                link(nc.vector.tensor_scalar(diff[:, 0:w], prob[:, 0, 0:w], rinv[:, 0:1], None, ALU.mult))
                nc.vector.scalar_tensor_tensor(out=diff[:, 0:w], in0=prob[:, 1, 0:w], scalar=rinv[:, 1:2],
                                               in1=diff[:, 0:w], op0=ALU.mult, op1=ALU.add).then_inc(diffed, 1)
                dve.wait_ge(diffed, u + 1)
            hh, tt0, _, qq = units[-1]
            take_output(len(units) - 1, hh, tt0 + qq)
            dve.wait_ge(o_ev, len(units))
            for t in range(NT):
                for h in range(H):
                    o = vf[:, t, 512 + h * P:512 + (h + 1) * P]
                    last = nc.vector.tensor_tensor_reduce(diags[:, 0, :], o, o, 1.0 / P, EPS, ALU.mult, ALU.add,
                                                          ssq[:, t * H + h:t * H + h + 1])
                    link(last)
            nc.vector.tensor_scalar(ssq, ssq, 0.0, None, ALU.add).then_inc(ssq_done, 1)
            dve.wait_ge(rms_done, 1)
            link(nc.vector.reciprocal(rrms, rms))
            for t in range(NT):
                for h in range(H):
                    o = vf[:, t, 512 + h * P:512 + (h + 1) * P]
                    last = nc.vector.scalar_tensor_tensor(out=o, in0=o, scalar=rrms[:, t * H + h:t * H + h + 1],
                                                          in1=sub_g, op0=ALU.mult, op1=ALU.mult)
                    if h < H - 1:
                        link(last)
                last.then_inc(o_norm, 1)
            for n in range(2 * NT):
                t, half = divmod(n, 2)
                dve.wait_ge(wo_mm, n + 1)
                r = xn[:, t, 512 * half:512 * half + 512]
                nc.vector.scalar_tensor_tensor(out=r, in0=r, scalar=ALPHA, in1=bank(n % 8),
                                               op0=ALU.mult, op1=ALU.add).then_inc(wo_add, 1)
                dve.wait_ge(wo_add, n + 1)
                if half:
                    ln_stats(t)
            ln_apply(1, x1_done)

            steps = [0]

            def step(ins):
                steps[0] += 1
                ins.then_inc(chain, 1)
                dve.wait_ge(chain, steps[0])

            def restart():
                dve.wait_ge(chain, steps[0])
                dve.sem_clear(chain)
                steps[0] = 0

            def retrieval(t, par):
                def begin():
                    dve.wait_ge(sc_cur, t + 1)
                    dve.sem_inc(scores_seen, 1)

                def top16(v, i, row):
                    for k in range(2):
                        v8 = v[:, 8 * k:8 * k + 8]
                        step(nc.vector.max(v8, row))
                        step(nc.vector.max_index(i[:, 8 * k:8 * k + 8], v8, row))
                        if k == 0:
                                step(nc.vector.match_replace(row, v8, row, NEG))

                def rows(r):
                    if r == 0:
                        begin()
                    top16(vals[:, r, :], iu[:, r, :], scur[:, r, :])

                def sums():
                    nc.vector.tensor_copy(idf, iu.rearrange("p r k -> p (r k)")).then_inc(sc_used, 1)
                    dve.wait_ge(sc_used, t + 1)
                    c4 = cand.rearrange("p (h a b) -> p h a b", h=PH, a=TOPK)
                    shape = [P, PH, TOPK, TOPK]
                    step(nc.vector.tensor_tensor(c4, vals[:, 0:PH, :].unsqueeze(3).broadcast_to(shape),
                                                 vals[:, PH:2 * PH, :].unsqueeze(2).broadcast_to(shape), ALU.add))

                def heads(h):
                    c = cand.rearrange("p (h n) -> p h n", h=PH)[:, h, :]
                    top16(best[:, h, :], posu[:, h, :], c)

                def positions():
                    flat = posu.rearrange("p h k -> p (h k)")
                    step(nc.vector.tensor_scalar(pshift, flat, 4, None, ALU.logical_shift_right))
                    step(nc.vector.tensor_copy(pabf[:, 0, :], pshift))
                    step(nc.vector.tensor_scalar(pshift, flat, TOPK - 1, None, ALU.bitwise_and))
                    step(nc.vector.tensor_copy(pabf[:, 1, :], pshift))

                def lookup(c, part):
                    p3 = pick.rearrange("p (s a) -> p s a", a=TOPK)
                    if part == 0:
                        step(nc.vector.tensor_tensor(
                            p3, pabf[:, c, :].unsqueeze(2).broadcast_to([P, NSLOT, TOPK]),
                            iota16.unsqueeze(1).broadcast_to([P, NSLOT, TOPK]), ALU.is_equal))
                    elif part == 1:
                        shape = [P, PH, TOPK, TOPK]
                        p4 = pick.rearrange("p (h k a) -> p h k a", h=PH, k=TOPK)
                        rows = idf.rearrange("p (r k) -> p r k", r=2 * PH)[:, c * PH:(c + 1) * PH, :]
                        step(nc.vector.tensor_tensor(p4, p4, rows.unsqueeze(2).broadcast_to(shape), ALU.mult))
                    else:
                        step(nc.vector.tensor_reduce(iab[:, c, :], p3, AX.X, ALU.add))

                def indices():
                    step(nc.vector.scalar_tensor_tensor(out=eidf, in0=iab[:, 0, :], scalar=float(NK),
                                                        in1=iab[:, 1, :], op0=ALU.mult, op1=ALU.add))
                    nc.vector.tensor_copy(idx[:, par, :], eidf).then_inc(idx_ready, 1)

                def gates_a():
                    step(nc.vector.tensor_copy(mx8, best[:, :, 0]))
                    nc.vector.tensor_tensor(best, best, mx8.unsqueeze(2).broadcast_to([P, PH, TOPK]),
                                            ALU.subtract).then_inc(best_sub, 1)

                def gates_b():
                    dve.wait_ge(gate_exp, t + 1)
                    step(nc.vector.tensor_reduce(gsum, best, AX.X, ALU.add))
                    step(nc.vector.reciprocal(gsum, gsum))
                    g3 = gate.rearrange("p (h k) -> p h k", h=PH)
                    step(nc.vector.tensor_tensor(g3, best, gsum.unsqueeze(2).broadcast_to([P, PH, TOPK]), ALU.mult))

                out_p = [lambda r=r: rows(r) for r in range(2 * PH)] + [sums]
                out_p += [lambda h=h: heads(h) for h in range(PH)] + [positions]
                out_p += [lambda c=c, k=k: lookup(c, k) for c in range(2) for k in range(3)]
                return out_p + [indices, gates_a, gates_b]

            def tile(t, par, last):
                dve.wait_ge(x_cur, t + 1)
                for s in range(NSLOT):
                    row = ring[:, s % RING, :]
                    dve.wait_ge(row_in[s % RING], use(t, s, 0) * 16)
                    nc.vector.tensor_tensor_reduce(row, row, xcur, 1.0, 0.0, ALU.mult, ALU.add,
                                                   act[:, s:s + 1]).then_inc(row_used[s % RING], 1)
                for k in range(RING):
                    dve.wait_ge(row_used[k], use(t, NSLOT - RING + k, 0) + 1)
                step(nc.vector.tensor_tensor(gt[0], act, act, ALU.mult))
                step(nc.vector.tensor_scalar(gt[0], gt[0], GELU_A, 1.0, ALU.mult, ALU.add))
                nc.vector.tensor_tensor(gt[0], gt[0], act, ALU.mult).then_inc(gelu_arg, 1)
                dve.wait_ge(gelu_exp, t + 1)
                step(nc.vector.tensor_scalar(gt[1], gt[1], 1.0, None, ALU.add))
                step(nc.vector.reciprocal(gt[1], gt[1]))
                step(nc.vector.tensor_tensor(gt[1], gt[1], act, ALU.mult))
                step(nc.vector.tensor_tensor(coef, gt[1], gate, ALU.mult))
                dve.wait_ge(y_stored, t + 1)
                nc.vector.tensor_scalar(acc, xcur, ALPHA, None, ALU.mult).then_inc(acc_init, 1)
                dve.wait_ge(acc_init, t + 1)
                pieces = [] if last else retrieval(t + 1, 1 - par)
                n = 0
                for s in range(NSLOT):
                    if s in V_PE:
                        if n >= 4:
                            q = V_PE[n - 4]
                            dve.wait_ge(row_used[q % RING], use(t, q, 1) + 1)
                        nc.vector.tensor_scalar(diags[:, n % 4, :], ident[:, :], coef[:, s:s + 1], None,
                                                ALU.mult).then_inc(diag_ready, 1)
                        n += 1
                    else:
                        if s >= V_ON_DVE:
                            dve.wait_ge(row_used[(s - V_ON_DVE) % RING], use(t, s - V_ON_DVE, 1) + 1)
                        dve.wait_ge(row_in[s % RING], use(t, s, 1) * 16)
                        nc.vector.scalar_tensor_tensor(out=acc, in0=ring[:, s % RING, :], scalar=coef[:, s:s + 1],
                                                       in1=acc, op0=ALU.mult, op1=ALU.add)\
                            .then_inc(row_used[s % RING], 1)
                    if pieces:
                        pieces.pop(0)()
                assert not pieces
                dve.wait_ge(row_used[(NSLOT - 1) % RING], use(t, NSLOT - 1, 1) + 1)
                dve.wait_ge(row_used[V_PE[-1] % RING], use(t, V_PE[-1], 1) + 1)
                nc.vector.tensor_tensor(acc, acc, wide[0][:, :], ALU.add).then_inc(y_taken, 1)
                dve.wait_ge(y_taken, t + 2)
                for j in range(2):
                    step(nc.vector.bn_stats(lnrow[:, 6 * j:6 * j + 6], acc[:, 512 * j:512 * j + 512]))
                step(nc.vector.bn_aggr(lnrow[:, 12:14], lnrow[:, 0:12]))
                nc.vector.tensor_scalar(lnrow[:, 14:15], lnrow[:, 13:14], EPS, None, ALU.add).then_inc(var2, 1)
                dve.wait_ge(std2, t + 1)
                step(nc.vector.reciprocal(lnrow[:, 16:17], lnrow[:, 15:16]))
                step(nc.vector.tensor_scalar(acc, acc, lnrow[:, 12:13], lnrow[:, 16:17], ALU.subtract, ALU.mult))
                step(nc.vector.tensor_tensor(acc, acc, g_row, ALU.mult))
                nc.vector.tensor_tensor(acc, acc, b_row, ALU.add).then_inc(y_ready, 1)
                restart()

            dve.wait_ge(iota_done, 2)
            for piece in retrieval(0, 0):
                piece()
            restart()
            dve.wait_ge(gain_in[2], 32)
            with dve.Fori(0, NT // 2 - 1) as i:
                for par in range(2):
                    tile(i * 2 + par, par, False)
            tile(NT - 2, 0, False)
            tile(NT - 1, 1, True)


def dft_tables(n, scale):
    a = 2.0 * np.pi * ((np.arange(n)[:, None] * np.arange(n)[None, :]) % n) / n
    return np.cos(a) * scale, np.sin(a) * scale


def kernel(**inputs):
    import numpy as _np
    import concourse.bacc as _bacc
    from concourse.bass_utils import run_bass_kernel_spmd as _run

    f = {k: _np.asarray(v) for k, v in inputs.items()}
    c, s = dft_tables(P, 1.0)
    arrays = {
        "x": _np.concatenate([f["x_prompt"][0], f["x_sample"][0]], axis=0),
        "ln_g": f["ln_in_g"], "ln_b": f["ln_in_b"], "w_in": f["w_in"][0],
        "lq1": f["lambda_q1"][0], "lk1": f["lambda_k1"][0], "lq2": f["lambda_q2"][0], "lk2": f["lambda_k2"][0],
        "subln_g": f["subln_g"][0], "w_f": f["w_fourier"][0], "b_f": f["b_fourier"][0], "w_out": f["w_out"][0],
        "ln1_g": f["ln1_g"][0], "ln1_b": f["ln1_b"][0], "wq": f["peer_wq"][0],
        "skt": _np.ascontiguousarray(f["peer_subkeys"][0].transpose(1, 3, 0, 2)).reshape(2, DQK, PH, NK),
        "pu": f["peer_u"][0], "pv": f["peer_v"][0], "ln2_g": f["ln2_g"][0], "ln2_b": f["ln2_b"][0],
        "dft_sample": _np.stack(dft_tables(S_SAMPLE, (S_SAMPLE * P) ** -0.5)).astype(_np.float32),
        "dft_prompt": _np.stack(dft_tables(S_PROMPT, (S_PROMPT * P) ** -0.5)).astype(_np.float32),
        "dft_chan": _np.stack([c, -s]).astype(_np.float32),
    }
    nc = _bacc.Bacc("TRN2", target_bir_lowering=False, num_devices=1)
    args, feed = [], {}
    for name, a in arrays.items():
        feed[f"in_{name}"] = _np.ascontiguousarray(a)
        args.append(nc.dram_tensor(f"in_{name}", a.shape, F32, kind="ExternalInput").ap())
    args.append(nc.dram_tensor("out_y", (T, D), F32, kind="ExternalOutput").ap())
    build(nc, *args)
    r = _run(nc, [feed], core_ids=[0])
    y = r.results[0]["out_y"]
    return y[None, :S_PROMPT], y[None, S_PROMPT:]
```

```python
from contextlib import ExitStack

import numpy as np

import concourse.bass as bass
from concourse import mybir

F32 = mybir.dt.float32
U32 = mybir.dt.uint32
F32R = mybir.dt.float32r
ALU = mybir.AluOpType
ACT = mybir.ActivationFunctionType
AX = mybir.AxisListType

P = 128
D = 1024
DC = D // P
S_PROMPT, S_SAMPLE = 256, 1024
NT = (S_PROMPT + S_SAMPLE) // P
T = NT * P
H = 4
HF = 4
DQK = 64
PH = 8
NK = 128
TOPK = 16
NSLOT = PH * TOPK
EPS = 1e-5
ALPHA = 2.0 ** 0.25
LAMBDA_INIT = 0.8 - 0.6
OUT_SCALE = 1.0 - LAMBDA_INIT
SLOPES = [2.0 ** (-8.0 * (h + 1) / H) for h in range(H)]
BATCHES = [(2, S_SAMPLE // P), (0, S_PROMPT // P)]
DIST_W = 2 * S_SAMPLE - P
RING = 4
NG = 4
ND = NT - NG
TD = ND * P
HN = TD // 2
NP = NK // 2
KP = NP // NG
SP_ = 2 * NSLOT // KP
GB_T = 4
NB = P // GB_T
assert KP * NG == NP and SP_ * KP == 2 * NSLOT and 2 * HN == TD and SP_ % RING == 0
NEG = -3.0e38


def token_blocks():
    return [(a, min(a + 512, T)) for a in range(0, T, 512)]


def build(nc, x, ln_g, ln_b, w_in, lq1, lk1, lq2, lk2, subln_g, w_f, b_f, w_out, ln1_g, ln1_b,
          wq, skt, pu, ut, pv, ln2_g, ln2_b, dft_sample, dft_prompt, dft_chan, gates, out):
    ctx = ExitStack()
    with ctx:
        origin = (nc.sbuf_base + 31) // 32 * 32

        def sb(name, at, cols, dt=F32):
            assert origin + 4 * (at + cols) <= nc.sbuf_usable_end
            return nc.alloc_sbuf_tensor_at(name, [P, cols], dt, offset=origin + 4 * at)

        def sem(name):
            return ctx.enter_context(nc.semaphore(name))

        BIG, XLN, QK, WB, GB, SM = 0, 20480, 30720, 40960, 49152, 51200
        big = sb("big", BIG, NT * 2 * D)
        xln = sb("xln", XLN, NT * D)
        qk = sb("qk", QK, DC * T)
        wbuf = sb("wbuf", WB, 8 * D)
        gb = sb("gb", GB, 2 * D)
        ident = sb("ident", SM, P)
        idx_sb = sb("idx_sb", SM + P, (NG + 1) * P, U32)
        small = sb("small", SM + (NG + 2) * P, 1200)
        xh_sb, xl_sb = sb("xh_sb", BIG, DC * TD, F32R), sb("xl_sb", BIG + DC * TD, DC * TD, F32R)
        a_at = BIG + 2 * DC * TD
        ah_sb, al_sb = sb("ah_sb", a_at, 4 * TD, F32R), sb("al_sb", a_at + 4 * TD, 4 * TD, F32R)
        g_sb = sb("g_sb", a_at + 8 * TD, 2 * TD)
        assert a_at + 10 * TD <= XLN
        uh_sb, ul_sb = sb("uh_sb", QK, 2 * D, F32R), sb("ul_sb", QK + 2 * D, 2 * D, F32R)
        vh_sb, vl_sb = sb("vh_sb", QK + 4 * D, 2 * D, F32R), sb("vl_sb", QK + 6 * D, 2 * D, F32R)
        peer_sb = sb("peer_sb", QK + 8 * D, 2 * D)

        xt = big[:, 0:DC * T].rearrange("p (c t) -> p c t", c=DC)
        vf = big[:, DC * T:].rearrange("p (t n) -> p t n", t=NT)
        sc = big[:, :].rearrange("p (t r) -> p t r", t=NT)
        xn = xln[:, :].rearrange("p (t n) -> p t n", t=NT)
        qkv = qk[:, :].rearrange("p (c t) -> p c t", c=DC)
        w8 = wbuf[:, :].rearrange("p (m c n) -> p m c n", m=8, c=DC)
        w2 = wbuf[:, :].rearrange("p (m c n) -> p m c n", m=2, c=DC)
        wfull = wbuf[:, :].rearrange("p (c n) -> p c n", c=DC)
        g_row, b_row = gb[:, 0:D], gb[:, D:2 * D]
        cc, scn = gb[:, 0:P], gb[:, P:2 * P]
        wf = gb[:, 2 * P:2 * P + HF * P].rearrange("p (g e) -> p g e", g=HF)
        bf = gb[:, 6 * P:6 * P + HF]
        trig = big[:, 0:4096].rearrange("p (k g s) -> p k g s", k=2, g=HF)
        zt = big[:, 4096:5120].rearrange("p (b s) -> p b s", b=2)
        dist = wbuf[:, 0:DIST_W]
        bias_h = wbuf[:, DIST_W:2 * DIST_W]
        o0 = 2 * DIST_W
        prob = wbuf[:, o0:o0 + 2 * D].rearrange("p (c k) -> p c k", c=2)
        diff = wbuf[:, o0 + 2 * D:o0 + 3 * D]
        difft = wbuf[:, o0 + 3 * D:o0 + 4 * D].rearrange("p (k q) -> p k q", k=8)
        assert o0 + 4 * D <= 8 * D
        sk = gb[:, 0:PH * NK].rearrange("p (h n) -> p h n", h=PH)

        n_small = [0]

        def sm(cols):
            a = n_small[0]
            n_small[0] += cols
            assert n_small[0] <= 1200
            return small[:, a:a + cols]

        stats = sm(NT * 12).rearrange("p (t s) -> p t s", t=NT)
        mv = sm(NT * 2).rearrange("p (t s) -> p t s", t=NT)
        veps = sm(NT)
        std = sm(NT)
        rstd = sm(NT)
        scratch = sm(P)
        gate = sm(NSLOT)
        iota_row = sm(P)
        n_mark = n_small[0]
        lam4 = sm(4 * DQK).rearrange("p (a d) -> p a d", a=4)
        sub_g = sm(P)
        lam2, elam, nlam = sm(2), sm(2), sm(1)
        rmax = sm(2)
        nrmax = sm(2)
        psum_row = sm(2)
        rinv = sm(2)
        ssq = sm(NT * H)
        rms = sm(NT * H)
        rrms = sm(NT * H)
        n_small[0] = n_mark
        iota16 = sm(TOPK)
        mx8 = sm(PH)
        best = sm(NSLOT).rearrange("p (h k) -> p h k", h=PH)
        gsum = sm(PH)

        at = [0]

        def wk(cols):
            a = at[0]
            at[0] += cols
            assert at[0] <= DC * T
            return qk[:, a:a + cols]

        scur = wk(2 * PH * NK).rearrange("p (r n) -> p r n", r=2 * PH)
        cand = wk(PH * TOPK * TOPK)
        pick = wk(NSLOT * TOPK)
        vals = wk(2 * PH * TOPK).rearrange("p (r k) -> p r k", r=2 * PH)
        idf = wk(2 * PH * TOPK)
        pabf = wk(2 * NSLOT).rearrange("p (c s) -> p c s", c=2)
        iab = wk(2 * NSLOT).rearrange("p (c s) -> p c s", c=2)
        eidf = wk(NSLOT)
        posu = wk(NSLOT).bitcast(U32).rearrange("p (h k) -> p h k", h=PH)
        pshift = wk(NSLOT).bitcast(U32)
        iu = wk(2 * PH * TOPK).bitcast(U32).rearrange("p (r k) -> p r k", r=2 * PH)
        hot = wk(16 * P).rearrange("p (w b n) -> p w b n", w=2, b=8)
        slot_t = wk(3 * P).rearrange("p (w t) -> p w t", w=3)
        idx = idx_sb[:, 0:NG * P].rearrange("p (t s) -> p t s", t=NG)
        idx_cur = idx_sb[:, NG * P:]
        spread = [wbuf[:, :].rearrange("p (j t) -> p j t", j=NK), big[:, 0:8 * D].rearrange("p (j t) -> p j t", j=NK)]
        xh = xh_sb[:, :].rearrange("p (c t) -> p c t", c=DC)
        xl = xl_sb[:, :].rearrange("p (c t) -> p c t", c=DC)
        ah = ah_sb[:, :].rearrange("p (b e t) -> p b e t", b=2, e=2)
        al = al_sb[:, :].rearrange("p (b e t) -> p b e t", b=2, e=2)
        uh = uh_sb[:, :].rearrange("p (e c i) -> p e c i", e=2, c=DC)
        ul = ul_sb[:, :].rearrange("p (e c i) -> p e c i", e=2, c=DC)
        vh = vh_sb[:, :].rearrange("p (e d) -> p e d", e=2)
        vl = vl_sb[:, :].rearrange("p (e d) -> p e d", e=2)
        g_in_sb = g_sb[:, :].rearrange("p (e t) -> p e t", e=2)
        ring = wbuf[:, 0:RING * D].rearrange("p (b n) -> p b n", b=RING)
        raw = wbuf[:, RING * D:].rearrange("p (w e n) -> p w e n", w=2, e=2)
        xcur = peer_sb[:, 0:D]
        act, coef, gact = (peer_sb[:, D + k * NSLOT:D + (k + 1) * NSLOT] for k in range(3))
        hid = gb[:, 0:2 * TD].rearrange("p (e t) -> p e t", e=2)
        gates_g = gb[:, 2 * TD:2 * TD + NG * NSLOT].rearrange("p (t s) -> p t s", t=NG)
        assert 2 * TD + NG * NSLOT <= 2 * D

        twin = [ctx.enter_context(nc.psum_tensor(f"twin{b}", [P, 1024], F32)) for b in range(4)]
        wide = twin[2:]
        act_psum = [t[:, :].rearrange("p (h n) -> p h n", h=2) for t in twin[:2]]

        def bank(n):
            return twin[n // 2][:, 512 * (n % 2):512 * (n % 2) + 512]

        x_in = [sem(f"x_in{t}") for t in range(NT)]
        gain_in = [sem(f"gain_in{k}") for k in range(3)]
        w_qk_in = [sem(f"w_qk_in{m}") for m in range(8)]
        w_vf_in = [sem(f"w_vf_in{m}") for m in range(2)]
        dft_in = [sem(f"dft_in{k}") for k in range(2)]
        four_in = sem("four_in")
        lam_in = sem("lam_in")
        w_out_in = sem("w_out_in")
        wq_in = [sem(f"wq_in{m}") for m in range(8)]
        sk_in = sem("sk_in")
        const_done = sem("const_done")
        dve_chain = sem("dve_chain")
        var_done = sem("var_done")
        std_done = sem("std_done")
        ln_in_done = sem("ln_in_done")
        xt_mm, xt_ev = sem("xt_mm"), sem("xt_ev")
        qk_mm, qk_ev = sem("qk_mm"), sem("qk_ev")
        vf_mm, vf_ev = sem("vf_mm"), sem("vf_ev")
        dft_mm, dft_ev = sem("dft_mm"), sem("dft_ev")
        z_mm, z_ev = sem("z_mm"), sem("z_ev")
        f_mm, f_ev = sem("f_mm"), sem("f_ev")
        lam_dots, lam_exp = sem("lam_dots"), sem("lam_exp")
        s_mm, biased, exped, diffed = sem("s_mm"), sem("biased"), sem("exped"), sem("diffed")
        at_mm, at_ev, pv_mm, o_ev = sem("at_mm"), sem("at_ev"), sem("pv_mm"), sem("o_ev")
        ssq_done, rms_done, o_norm = sem("ssq_done"), sem("rms_done"), sem("o_norm")
        ot_mm, ot_ev = sem("ot_mm"), sem("ot_ev")
        wo_mm, wo_add = sem("wo_mm"), sem("wo_add")
        x1_done = sem("x1_done")
        x1t_mm, x1t_ev = sem("x1t_mm"), sem("x1t_ev")
        wq_mm, wq_ev = sem("wq_mm"), sem("wq_ev")
        sc_mm, sc_ev = sem("sc_mm"), sem("sc_ev")
        iota_done = sem("iota_done")
        sc_cur = sem("sc_cur")
        chain = sem("chain")
        scores_seen, slots_free = sem("scores_seen"), sem("slots_free")
        sc_used, best_sub, gate_exp = sem("sc_used"), sem("best_sub"), sem("gate_exp")
        retrieved = sem("retrieved")
        turn_mm, turn_ev = sem("turn_mm"), sem("turn_ev")
        hot_i, hot_j = sem("hot_i"), sem("hot_j")
        g_mm, g_ev = sem("g_mm"), sem("g_ev")
        g_out, g_free = sem("g_out"), sem("g_free")
        xh_mm, xh_ev, xl_ev = sem("xh_mm"), sem("xh_ev"), sem("xl_ev")
        u_in = [sem(f"u_in{e}") for e in range(2)]
        v_in = [sem(f"v_in{e}") for e in range(2)]
        g_in = [sem(f"g_in{e}") for e in range(2)]
        uh_done, ul_done = sem("uh_done"), sem("ul_done")
        vh_done, vl_done = sem("vh_done"), sem("vl_done")
        h_mm, hid_done = sem("h_mm"), sem("hid_done")
        gated, ah_done, al_done = sem("gated"), sem("ah_done"), sem("al_done")
        y_mm, y_add = sem("y_mm"), sem("y_add")
        started = sem("started")
        x_cur, idx_copied, y_init = sem("x_cur"), sem("idx_copied"), sem("y_init")
        acts, gacts, coefs = sem("acts"), sem("gacts"), sem("coefs")
        row_in = [sem(f"row_in{k}") for k in range(RING)]
        row_used = [sem(f"row_used{k}") for k in range(RING)]
        y_done, y_out = sem("y_done"), sem("y_out")

        block = ctx.enter_context(nc.Block())

        USES = 2 * NSLOT // RING

        def use(t, s, v):
            return t * USES + (v * NSLOT + s) // RING + 1

        @block.sync
        def _(sp):
            for t in range(NT):
                sp.dma_start(xn[:, t, :], x[t * P:(t + 1) * P, :]).then_inc(x_in[t], 16)
                if t == 1:
                    sp.dma_start(g_row, ln_g.partition_broadcast(P)).then_inc(gain_in[0], 16)
                    sp.dma_start(b_row, ln_b.partition_broadcast(P)).then_inc(gain_in[0], 16)
            w_in_v = w_in.rearrange("(c p) n -> p c n", p=P)
            for m in range(8):
                sp.dma_start(w8[:, m], w_in_v[:, :, m * P:(m + 1) * P]).then_inc(w_qk_in[m], 16)
            for a, v in enumerate((lq1, lk1, lq2, lk2)):
                sp.dma_start(lam4[:, a, :], v.partition_broadcast(P)).then_inc(lam_in, 16)
            sp.dma_start(sub_g, subln_g.partition_broadcast(P)).then_inc(lam_in, 16)
            blocks = len(token_blocks())
            for m in range(2):
                sp.wait_ge(qk_mm, 4 * (m + 1) * blocks)
                sp.dma_start(w2[:, m], w_in_v[:, :, D + 512 * m:D + 512 * (m + 1)]).then_inc(w_vf_in[m], 16)
            sp.wait_ge(ln_in_done, NT)
            sp.dma_start(cc, dft_chan[0]).then_inc(four_in, 16)
            sp.dma_start(scn, dft_chan[1]).then_inc(four_in, 16)
            sp.dma_start(wf, w_f.rearrange("g c e -> c g e")).then_inc(four_in, 16)
            sp.dma_start(bf, b_f.rearrange("g e -> e g"), allow_slow_non_contiguous=True).then_inc(four_in, 16)
            for n in range(3):
                for k in range(2):
                    if n == 0:
                        sp.wait_ge(vf_mm, NT * (k + 1))
                    else:
                        sp.wait_ge(dft_mm, 2 * HF * (n - 1) + HF * (k + 1))
                    if n < 2:
                        sp.dma_start(w2[:, k], dft_sample[k].rearrange("(c p) s -> p c s", p=P)[
                            :, :, 512 * n:512 * n + 512]).then_inc(dft_in[k], 16)
                    else:
                        sp.dma_start(w2[:, k, 0:2, 0:S_PROMPT],
                                     dft_prompt[k].rearrange("(c p) s -> p c s", p=P)).then_inc(dft_in[k], 16)
            sp.wait_ge(f_mm, 3 * HF)
            sp.wait_ge(f_ev, 3 * HF)
            sp.dma_start(g_row, ln1_g.partition_broadcast(P)).then_inc(gain_in[1], 16)
            sp.dma_start(b_row, ln1_b.partition_broadcast(P)).then_inc(gain_in[1], 16)
            sp.wait_ge(pv_mm, NT * H)
            sp.wait_ge(diffed, NT * H)
            sp.dma_start(wfull, w_out.rearrange("(c p) n -> p c n", p=P)).then_inc(w_out_in, 16)
            sp.wait_ge(wo_mm, 2 * NT)
            wq_v = wq.rearrange("(c p) n -> p c n", p=P)
            for m in range(8):
                sp.dma_start(w8[:, m], wq_v[:, :, m * P:(m + 1) * P]).then_inc(wq_in[m], 16)
            sp.wait_ge(x1_done, NT)
            sp.dma_start(sk, skt.rearrange("c d h n -> (c d) h n")).then_inc(sk_in, 16)
            sp.wait_ge(sc_mm, 4 * NT)
            g_by_i = gates.rearrange("j i t -> i j t")
            sp.sem_inc(g_free, 2)
            with sp.Fori(0, ND) as i:
                for m in range(2):
                    sp.wait_ge(g_ev, i * NB + (NB // 2 * (m + 1) + 4))
                    sp.dma_start(g_by_i[:, :, bass.ds(i * P + 64 * m, 64)], spread[m]).then_inc(g_out, 16)
                    sp.wait_ge(g_out, i * 32 + 16 * (m + 1))
                    sp.sem_inc(g_free, 1)
            v_by_j = pv.rearrange("(i j) d -> j i d", j=NK)
            with sp.Fori(0, NP) as q:
                for e in range(2):
                    sp.wait_ge(ul_done, q * 2 + e + 1)
                    sp.dma_start(raw[:, 0, e, :], ut[bass.ds(q * 2 + e, 1), :, :].rearrange("a p n -> (a p) n"))\
                        .then_inc(u_in[e], 16)
                for e in range(2):
                    sp.wait_ge(gated, q * 2 + e + 1)
                    sp.dma_start(g_in_sb[:, e, :], gates[bass.ds(q * 2 + e, 1), :, :].rearrange("a p n -> (a p) n"))\
                        .then_inc(g_in[e], 16)
                for e in range(2):
                    sp.wait_ge(vl_done, q * 2 + e + 1)
                    sp.dma_start(raw[:, 1, e, :], v_by_j[bass.ds(q * 2 + e, 1), :, :].rearrange("a p n -> (a p) n"))\
                        .then_inc(v_in[e], 16)
            sp.wait_ge(y_add, ND * NP + ND)
            sp.wait_ge(gated, 2 * NP + 2)
            sp.wait_ge(coefs, 2 * NG)
            sp.wait_ge(al_done, 2 * NP + 2)
            sp.dma_start(g_row, ln2_g.partition_broadcast(P)).then_inc(gain_in[2], 16)
            sp.dma_start(b_row, ln2_b.partition_broadcast(P)).then_inc(gain_in[2], 16)
            for t in range(NT):
                sp.wait_ge(y_done, t + 1)
                sp.dma_start(out[t * P:(t + 1) * P, :], xn[:, t, :]).then_inc(y_out, 16)
            sp.wait_ge(y_out, 16 * NT)

        @block.gpsimd
        def _(pool):
            pool.memset(ident[:, :], 0.0).then_inc(const_done, 1)
            pool.wait_ge(const_done, 1)
            pool.affine_select(out=ident[:, :], in_=ident[:, :], compare_op=ALU.not_equal, fill=1.0, base=0,
                               pattern=[[-1, P]], channel_multiplier=1).then_inc(const_done, 1)
            pool.wait_ge(dft_mm, 3 * 2 * HF)
            pool.iota(dist, pattern=[[-1, DIST_W]], base=S_SAMPLE - P, channel_multiplier=1,
                      allow_small_or_imprecise_dtypes=True).then_inc(iota_done, 1)
            pool.wait_ge(o_norm, NT)
            pool.wait_ge(ot_ev, NT)
            pool.iota(iota16, pattern=[[1, TOPK]], base=0, channel_multiplier=0,
                      allow_small_or_imprecise_dtypes=True).then_inc(iota_done, 1)
            pool.iota(iota_row, pattern=[[1, P]], base=0, channel_multiplier=0,
                      allow_small_or_imprecise_dtypes=True).then_inc(iota_done, 1)
            pool.wait_ge(iota_done, 3)
            with pool.Fori(0, ND) as i:
                pool.wait_ge(turn_ev, i + 1)
                for b in range(NB):
                    pool.wait_ge(g_mm, i * NB + b + 1)
                    pool.sem_inc(slots_free, 1)
                    for k in range(GB_T):
                        last = pool.tensor_scalar(hot[:, 1, 4 * (b % 2) + k, :], iota_row,
                                                  slot_t[:, 1, GB_T * b + k:GB_T * b + k + 1], None, ALU.is_equal)
                    last.then_inc(hot_j, 1)

            def lo_part(which, c, e):
                hi, lo, ready, done, used = ((uh_sb, ul_sb, uh_done, ul_done, h_mm),
                                             (vh_sb, vl_sb, vh_done, vl_done, y_mm))[which]
                pool.wait_ge(ready, c + 1)
                cols = slice(e * D, (e + 1) * D)
                pool.tensor_tensor(lo[:, cols], raw[:, which, e, :], hi[:, cols].bitcast(F32), ALU.subtract)\
                    .then_inc(done, 1)

            def tile(g, first, last):
                if not first:
                    pool.wait_ge(row_used[RING - 1], use(g, 0, 0))
                    pool.sem_inc(slots_free, 1)
                pool.tensor_copy(idx_cur, idx[:, bass.ds(g, 1), :].rearrange("p a s -> p (a s)"))\
                    .then_inc(idx_copied, 1)
                pool.wait_ge(idx_copied, g + 1)
                pool.sem_inc(slots_free, 1)
                for k in range(KP):
                    q = g * KP + k
                    for part in range(4):
                        for n in range(SP_ // 4):
                            s = k * SP_ + part * (SP_ // 4) + n
                            v, slot = divmod(s, NSLOT)
                            pool.wait_ge(row_used[s % RING], use(g, slot, v))
                            pool.sem_inc(slots_free, 1)
                            pool.indirect_dma_start(
                                ring[:, s % RING, :], None, (pu, pv)[v],
                                bass.IndirectOffsetOnAxis(ap=idx_cur[:, slot:slot + 1], axis=0))\
                                .then_inc(row_in[s % RING], 16)
                        if part < 2:
                            if not (last and k == KP - 1):
                                lo_part(0, q * 2 + 2 + part, part)
                        else:
                            lo_part(1, q * 2 + (part - 2), part - 2)

            pool.wait_ge(started, 1)
            for k in range(RING):
                pool.sem_inc(row_used[k], 1)
            pool.sem_inc(ul_done, 2)
            pool.sem_inc(vl_done, 2)
            for e in range(2):
                lo_part(0, e, e)
            tile(0, True, False)
            with pool.Fori(1, NG - 1) as g:
                tile(g, False, False)
            tile(NG - 1, False, True)

        def att_groups(u, k):
            per_head = sum(nt * ((nt + 3) // 4) for _, nt in BATCHES)
            h, r = divmod(u, NT)
            n = h * per_head
            for _, nt in BATCHES:
                g = (nt + 3) // 4
                if r < nt:
                    return n + r * g + k // 4
                n += nt * g
                r -= nt

        @block.scalar
        def _(act_e):
            def evac(dst, src, func=ACT.Copy, **kw):
                return nc.scalar.activation(dst, src, func, **kw)

            act_e.wait_ge(var_done, 1)
            nc.scalar.activation(std, veps, ACT.Sqrt).then_inc(std_done, 1)
            for n in range(2 * NT):
                t, half = divmod(n, 2)
                act_e.wait_ge(xt_mm, n + 1)
                evac(xt[:, 4 * half:4 * half + 4, t * P:(t + 1) * P],
                     bank(n % 8).rearrange("p (c t) -> p c t", c=4)).then_inc(xt_ev, 1)
            n = 0
            for m in range(8):
                for a, b in token_blocks():
                    act_e.wait_ge(qk_mm, n + 1)
                    evac(qkv[:, m, a:b], bank(n % 8)[:, 0:b - a], scale=DQK ** -0.5 if m < 4 else 1.0)\
                        .then_inc(qk_ev, 1)
                    n += 1
            n = 0
            for m in range(2):
                for t in range(NT):
                    act_e.wait_ge(vf_mm, n + 1)
                    evac(vf[:, t, 512 * m:512 * m + 512], bank(n % 8)).then_inc(vf_ev, 1)
                    n += 1
            act_e.wait_ge(lam_dots, 1)
            nc.scalar.activation(elam, lam2, ACT.Exp).then_inc(lam_exp, 1)
            act_e.wait_ge(four_in, 64)
            for n in range(3):
                w = 512 if n < 2 else S_PROMPT
                tok = S_PROMPT + 512 * n if n < 2 else 0
                for j in range(2 * HF):
                    act_e.wait_ge(dft_mm, 2 * HF * n + j + 1)
                    if n > 0:
                        act_e.wait_ge(z_mm, HF * n)
                    evac(trig[:, j // HF, j % HF, 0:w], bank(j % 4)[:, 0:w]).then_inc(dft_ev, 1)
                for g in range(HF):
                    m = HF * n + g
                    act_e.wait_ge(z_mm, m + 1)
                    if m >= 2:
                        act_e.wait_ge(f_mm, m - 1)
                    evac(zt[:, m % 2, 0:w], bank(4 + m % 2)[:, 0:w]).then_inc(z_ev, 1)
                    act_e.wait_ge(f_mm, m + 1)
                    nc.scalar.activation(xt[:, 4 + g, tok:tok + w], bank(6 + m % 2)[:, 0:w], ACT.Identity,
                                         bias=bf[:, g:g + 1]).then_inc(f_ev, 1)
            u = 0
            for h in range(H):
                for t0, nt in BATCHES:
                    for qt in range(nt):
                        for c in range(2):
                            act_e.wait_ge(biased, 2 * u + c + 1)
                            keys = prob[:, c, 0:nt * P]
                            nc.scalar.activation(keys, keys, ACT.Exp, bias=nrmax[:, c:c + 1],
                                                 accum_out=psum_row[:, c:c + 1]).then_inc(exped, 1)
                        for k in range(0, nt, 4):
                            n = min(4, nt - k)
                            act_e.wait_ge(at_mm, att_groups(u, k) + 1)
                            if u:
                                act_e.wait_ge(pv_mm, u)
                            evac(difft[:, k:k + n, :], bank(k // 4)[:, 0:n * P].rearrange("p (k q) -> p k q", q=P))\
                                .then_inc(at_ev, 1)
                        u += 1
            act_e.wait_ge(ssq_done, 1)
            nc.scalar.activation(rms, ssq, ACT.Sqrt).then_inc(rms_done, 1)
            for t in range(NT):
                act_e.wait_ge(ot_mm, t + 1)
                evac(xt[:, 0:4, t * P:(t + 1) * P], bank(t % 8).rearrange("p (c t) -> p c t", c=4))\
                    .then_inc(ot_ev, 1)
            act_e.wait_ge(var_done, 2)
            nc.scalar.activation(std, veps, ACT.Sqrt).then_inc(std_done, 1)
            act_e.wait_ge(wo_mm, 2 * NT)
            for n in range(2 * NT):
                t, half = divmod(n, 2)
                act_e.wait_ge(x1t_mm, n + 1)
                evac(xt[:, 4 * half:4 * half + 4, t * P:(t + 1) * P],
                     bank(n % 8).rearrange("p (c t) -> p c t", c=4)).then_inc(x1t_ev, 1)
            n = 0
            for m in range(8):
                for a, b in token_blocks():
                    act_e.wait_ge(wq_mm, n + 1)
                    evac(qkv[:, m, a:b], bank(n % 8)[:, 0:b - a]).then_inc(wq_ev, 1)
                    n += 1
            for n in range(4 * NT):
                act_e.wait_ge(sc_mm, n + 1)
                evac(sc[:, n // 4, 512 * (n % 4):512 * (n % 4) + 512], bank(n % 8)).then_inc(sc_ev, 1)

            def load_scores(t):
                evac(scur.rearrange("p r n -> p (r n)"), sc[:, bass.ds(t, 1), :].rearrange("p a r -> p (a r)"))\
                    .then_inc(sc_cur, 1)

            def gate_exps(t):
                act_e.wait_ge(best_sub, t + 1)
                flat = best.rearrange("p h k -> p (h k)")
                nc.scalar.activation(flat, flat, ACT.Exp).then_inc(gate_exp, 1)

            act_e.wait_ge(sc_ev, 4 * NT)
            load_scores(0)
            with act_e.Fori(0, NG) as t:
                gate_exps(t)
                act_e.wait_ge(sc_used, t + 1)
                load_scores(t + 1)
            gate_exps(NG)

            def spread_tile(i, last):
                act_e.wait_ge(turn_mm, i + 1)
                act_e.wait_ge(g_mm, i * NB + 2)
                evac(slot_t, bank(0)[:, 0:3 * P].rearrange("p (w t) -> p w t", w=3)).then_inc(turn_ev, 1)
                if not last:
                    act_e.wait_ge(sc_used, i + (NG + 1))
                    load_scores(i + (NG + 1))
                for b in range(NB):
                    if b % (NB // 2) == 0:
                        act_e.wait_ge(g_free, i * 2 + b // (NB // 2) + 1)
                    act_e.wait_ge(g_mm, i * NB + b + 3)
                    t0 = GB_T * (b % (NB // 2))
                    evac(spread[b // (NB // 2)][:, :, t0:t0 + GB_T],
                         bank(4 + b % 4).rearrange("p (t j) -> p j t", t=GB_T)).then_inc(g_ev, 1)
                if not last:
                    gate_exps(i + (NG + 1))

            act_e.sem_inc(g_ev, 4)
            act_e.sem_inc(hid_done, 2)
            with act_e.Fori(0, ND - 1) as i:
                spread_tile(i, False)
            spread_tile(ND - 1, True)

            for n in range(2 * ND):
                t, half = divmod(n, 2)
                act_e.wait_ge(xh_mm, n + 1)
                evac(xh[:, 4 * half:4 * half + 4, t * P:(t + 1) * P],
                     bank(n % 8).rearrange("p (c t) -> p c t", c=4)).then_inc(xh_ev, 1)

            def hi_part(which, q, e):
                c = q * 2 + e
                if which == 0:
                    act_e.wait_ge(h_mm, c + 1)
                    act_e.wait_ge(u_in[e], q * 16 + 16)
                    evac(uh_sb[:, e * D:(e + 1) * D], raw[:, 0, e, :]).then_inc(uh_done, 1)
                else:
                    act_e.wait_ge(y_mm, q * ND + 2 * ND)
                    act_e.wait_ge(v_in[e], q * 16 + 16)
                    evac(vh_sb[:, e * D:(e + 1) * D], raw[:, 1, e, :]).then_inc(vh_done, 1)

            def peer_tile(g, last):
                evac(xcur, xn[:, bass.ds(g, 1), :].rearrange("p a n -> p (a n)")).then_inc(x_cur, 1)
                for k in range(KP):
                    q = g * KP + k
                    for e in range(2):
                        c = q * 2 + e
                        act_e.wait_ge(h_mm, c + 3)
                        act_e.wait_ge(al_done, c + 1)
                        evac(hid[:, e, :].rearrange("p (h t) -> p h t", h=2),
                             act_psum[e][:, :, 0:HN], ACT.Gelu_apprx_tanh).then_inc(hid_done, 1)
                        if not (last and k == KP - 1):
                            hi_part(0, q + 1, e)
                    for e in range(2):
                        c = q * 2 + e
                        act_e.wait_ge(gated, c + 3)
                        if e == 0:
                            act_e.wait_ge(y_mm, q * ND + ND)
                        evac(ah[:, k % 2, e, :], hid[:, e, :]).then_inc(ah_done, 1)
                    for e in range(2):
                        hi_part(1, q, e)
                    if k == KP // 2 - 1:
                        act_e.wait_ge(acts, g + 1)
                        evac(gact, act, ACT.Gelu_apprx_tanh).then_inc(gacts, 1)
                act_e.wait_ge(coefs, g * 2 + 2)

            act_e.wait_ge(started, 1)
            for e in range(2):
                act_e.wait_ge(u_in[e], 16)
                evac(uh_sb[:, e * D:(e + 1) * D], raw[:, 0, e, :]).then_inc(uh_done, 1)
            with act_e.Fori(0, NG - 1) as g:
                peer_tile(g, False)
            peer_tile(NG - 1, True)
            act_e.wait_ge(var_done, 3)
            nc.scalar.activation(std, veps, ACT.Sqrt).then_inc(std_done, 1)

        @block.tensor
        def _(pe):
            pe.wait_ge(const_done, 2)
            for n in range(2 * NT):
                t, half = divmod(n, 2)
                if half == 0:
                    pe.wait_ge(ln_in_done, t + 1)
                if n >= 8:
                    pe.wait_ge(xt_ev, n - 7)
                for c in range(4):
                    j = 4 * half + c
                    last = nc.tensor.transpose(bank(n % 8)[:, c * P:(c + 1) * P], xn[:, t, j * P:(j + 1) * P],
                                               ident[:, :])
                last.then_inc(xt_mm, 1)
            pe.wait_ge(xt_ev, 2 * NT)
            n = 0
            for m in range(8):
                pe.wait_ge(w_qk_in[m], 16)
                for a, b in token_blocks():
                    if n >= 8:
                        pe.wait_ge(qk_ev, n - 7)
                    for c in range(DC):
                        last = nc.tensor.matmul(bank(n % 8)[:, 0:b - a], w8[:, m, c, :], xt[:, c, a:b],
                                                start=(c == 0), stop=(c == DC - 1))
                    last.then_inc(qk_mm, 1)
                    n += 1
            pe.wait_ge(qk_ev, 8 * len(token_blocks()))
            n = 0
            for m in range(2):
                pe.wait_ge(w_vf_in[m], 16)
                for t in range(NT):
                    if n >= 8:
                        pe.wait_ge(vf_ev, n - 7)
                    for c in range(DC):
                        last = nc.tensor.matmul(bank(n % 8), xt[:, c, t * P:(t + 1) * P], w2[:, m, c, :],
                                                start=(c == 0), stop=(c == DC - 1))
                    last.then_inc(vf_mm, 1)
                    n += 1
            pe.wait_ge(vf_ev, 2 * NT)
            pe.wait_ge(four_in, 64)
            for n in range(3):
                w, t0, nc_k = (512, 2, 8) if n < 2 else (S_PROMPT, 0, 2)
                for j in range(2 * HF):
                    k, g = divmod(j, HF)
                    if g == 0:
                        pe.wait_ge(dft_in[k], 16 * (n + 1))
                    if 2 * HF * n + j >= 4:
                        pe.wait_ge(dft_ev, 2 * HF * n + j - 3)
                    for c in range(nc_k):
                        last = nc.tensor.matmul(bank(j % 4)[:, 0:w], vf[:, t0 + c, 512 + g * P:512 + (g + 1) * P],
                                                w2[:, k, c, 0:w], start=(c == 0), stop=(c == nc_k - 1))
                    last.then_inc(dft_mm, 1)
                for g in range(HF):
                    m = HF * n + g
                    pe.wait_ge(dft_ev, 2 * HF * n + HF + g + 1)
                    if m >= 2:
                        pe.wait_ge(z_ev, m - 1)
                    nc.tensor.matmul(bank(4 + m % 2)[:, 0:w], cc, trig[:, 0, g, 0:w], start=True, stop=False)
                    nc.tensor.matmul(bank(4 + m % 2)[:, 0:w], scn, trig[:, 1, g, 0:w], start=False, stop=True)\
                        .then_inc(z_mm, 1)
                    pe.wait_ge(z_ev, m + 1)
                    if m >= 2:
                        pe.wait_ge(f_ev, m - 1)
                    nc.tensor.matmul(bank(6 + m % 2)[:, 0:w], wf[:, g, :], zt[:, m % 2, 0:w],
                                     start=True, stop=True).then_inc(f_mm, 1)
            pe.wait_ge(f_ev, 3 * HF)

            units = [(h, t0, nt, qt) for h in range(H) for t0, nt in BATCHES for qt in range(nt)]

            def scores(u):
                h, t0, nt, qt = units[u]
                q0, k0 = (t0 + qt) * P, t0 * P
                for c in range(2):
                    if u:
                        pe.wait_ge(biased, 2 * (u - 1) + c + 1)
                    rows = slice(c * DQK, (c + 1) * DQK)
                    for k in range(0, nt * P, 512):
                        w = min(512, nt * P - k)
                        last = nc.tensor.matmul(wide[c][:, k:k + w], qkv[rows, h, q0:q0 + P],
                                                qkv[rows, 4 + h, k0 + k:k0 + k + w], start=True, stop=True)
                    last.then_inc(s_mm, 1)

            def mix_values(u):
                h, t0, nt, qt = units[u]
                pe.wait_ge(diffed, u + 1)
                for k in range(0, nt, 4):
                    if att_groups(u, k) >= 1:
                        pe.wait_ge(at_ev, max(1, att_groups(u, 0)))
                    for j in range(k, min(k + 4, nt)):
                        last = nc.tensor.transpose(bank(k // 4)[:, (j - k) * P:(j - k + 1) * P],
                                                   diff[:, j * P:(j + 1) * P], ident[:, :])
                    last.then_inc(at_mm, 1)
                for j in range(nt):
                    if j % 4 == 0:
                        pe.wait_ge(at_ev, att_groups(u, j) + 1)
                    if u >= 2 and j == 0:
                        pe.wait_ge(o_ev, u - 1)
                    last = nc.tensor.matmul(bank(2 + u % 2)[:, 0:P], difft[:, j, :], vf[:, t0 + j, h * P:(h + 1) * P],
                                            start=(j == 0), stop=(j == nt - 1))
                last.then_inc(pv_mm, 1)

            scores(0)
            for u in range(len(units)):
                if u + 1 < len(units):
                    scores(u + 1)
                mix_values(u)
            for t in range(NT):
                pe.wait_ge(o_norm, t + 1)
                if t >= 8:
                    pe.wait_ge(ot_ev, t - 7)
                for h in range(H):
                    last = nc.tensor.transpose(bank(t % 8)[:, h * P:(h + 1) * P],
                                               vf[:, t, 512 + h * P:512 + (h + 1) * P], ident[:, :])
                last.then_inc(ot_mm, 1)
            pe.wait_ge(w_out_in, 16)
            pe.wait_ge(ot_ev, NT)
            for n in range(2 * NT):
                t, half = divmod(n, 2)
                if n >= 8:
                    pe.wait_ge(wo_add, n - 7)
                for c in range(DC):
                    last = nc.tensor.matmul(bank(n % 8), xt[:, c, t * P:(t + 1) * P],
                                            wfull[:, c, 512 * half:512 * half + 512],
                                            start=(c == 0), stop=(c == DC - 1))
                last.then_inc(wo_mm, 1)
            pe.wait_ge(wo_add, 2 * NT)
            for n in range(2 * NT):
                t, half = divmod(n, 2)
                if half == 0:
                    pe.wait_ge(x1_done, t + 1)
                if n >= 8:
                    pe.wait_ge(x1t_ev, n - 7)
                for c in range(4):
                    j = 4 * half + c
                    last = nc.tensor.transpose(bank(n % 8)[:, c * P:(c + 1) * P], xn[:, t, j * P:(j + 1) * P],
                                               ident[:, :])
                last.then_inc(x1t_mm, 1)
            pe.wait_ge(x1t_ev, 2 * NT)
            n = 0
            for m in range(8):
                pe.wait_ge(wq_in[m], 16)
                for a, b in token_blocks():
                    if n >= 8:
                        pe.wait_ge(wq_ev, n - 7)
                    for c in range(DC):
                        last = nc.tensor.matmul(bank(n % 8)[:, 0:b - a], w8[:, m, c, :], xt[:, c, a:b],
                                                start=(c == 0), stop=(c == DC - 1))
                    last.then_inc(wq_mm, 1)
                    n += 1
            pe.wait_ge(wq_ev, 8 * len(token_blocks()))
            pe.wait_ge(sk_in, 16)
            for n in range(4 * NT):
                t, c, h4 = n // 4, (n % 4) // 2, n % 2
                if n >= 8:
                    pe.wait_ge(sc_ev, n - 7)
                rows = slice(c * DQK, (c + 1) * DQK)
                for j in range(4):
                    h = 4 * h4 + j
                    last = nc.tensor.matmul(bank(n % 8)[:, j * NK:(j + 1) * NK], qkv[rows, h, t * P:(t + 1) * P],
                                            sk[rows, h, :], start=True, stop=True)
                last.then_inc(sc_mm, 1)
            pe.wait_ge(sc_ev, 4 * NT)

            pe.sem_inc(g_mm, 2)
            pe.sem_inc(h_mm, 2)
            pe.sem_inc(y_mm, 2 * ND)
            with pe.Fori(0, ND) as i:
                pe.wait_ge(retrieved, i + (NG + 1))
                for w, m in enumerate((iab[:, 0, :], iab[:, 1, :], gate)):
                    last = nc.tensor.transpose(bank(0)[:, w * P:(w + 1) * P], m, ident[:, :])
                last.then_inc(turn_mm, 1)
                for b in range(NB):
                    pe.wait_ge(hot_i, i * NB + b + 1)
                    pe.wait_ge(hot_j, i * NB + b + 1)
                    pe.wait_ge(g_ev, i * NB + b + 1)
                    for k in range(GB_T):
                        r = 4 * (b % 2) + k
                        last = nc.tensor.matmul(bank(4 + b % 4)[:, k * P:(k + 1) * P], hot[:, 0, r, :],
                                                hot[:, 1, r, :], start=True, stop=True)
                    last.then_inc(g_mm, 1)
            pe.wait_ge(g_free, 2 * ND + 2)
            for n in range(2 * ND):
                t, half = divmod(n, 2)
                if n >= 8:
                    pe.wait_ge(xl_ev, n - 7)
                else:
                    pe.wait_ge(g_ev, ND * NB + 4)
                for c in range(4):
                    j = 4 * half + c
                    last = nc.tensor.transpose(bank(n % 8)[:, c * P:(c + 1) * P], xn[:, NG + t, j * P:(j + 1) * P],
                                               ident[:, :])
                last.then_inc(xh_mm, 1)
            pe.wait_ge(xl_ev, 2 * ND)

            def activations(q, e):
                c = q * 2 + e
                pe.wait_ge(uh_done, c + 1)
                pe.wait_ge(ul_done, c + 3)
                pe.wait_ge(hid_done, c + 1)
                for k in range(DC):
                    for lhs, rhs in ((uh, xh), (uh, xl), (ul, xh)):
                        for h in range(2):
                            last = nc.tensor.matmul(
                                act_psum[e][:, h, 0:HN], lhs[:, e, k, :], rhs[:, k, h * HN:(h + 1) * HN],
                                start=(k == 0 and rhs is xh and lhs is uh), stop=(k == DC - 1 and lhs is ul))
                last.then_inc(h_mm, 1)

            def sums(q, par):
                pe.wait_ge(ah_done, q * 2 + 2)
                pe.wait_ge(al_done, q * 2 + 4)
                pe.wait_ge(vh_done, q * 2 + 2)
                pe.wait_ge(vl_done, q * 2 + 4)
                for t in range(ND):
                    pe.wait_ge(y_add, q * ND + t + (ND - 1))
                    toks = slice(t * P, (t + 1) * P)
                    for e in range(2):
                        for n, (lhs, rhs) in enumerate(((ah, vh), (ah, vl), (al, vh))):
                            for h in range(2):
                                last = nc.tensor.matmul(
                                    wide[t % 2][:, 512 * h:512 * h + 512], lhs[:, par, e, toks],
                                    rhs[:, e, 512 * h:512 * h + 512], start=(e == 0 and n == 0),
                                    stop=(e == 1 and n == 2))
                    last.then_inc(y_mm, 1)

            for e in range(2):
                activations(0, e)
            with pe.Fori(0, NP // 2 - 1) as i:
                for par in range(2):
                    for e in range(2):
                        activations(i * 2 + (par + 1), e)
                    sums(i * 2 + par, par)
            for e in range(2):
                activations(NP - 1, e)
            sums(NP - 2, 0)
            sums(NP - 1, 1)

        @block.vector
        def _(dve):
            done = [0]

            def link(ins):
                done[0] += 1
                ins.then_inc(dve_chain, 1)
                dve.wait_ge(dve_chain, done[0])

            def ln_stats(t):
                for j in range(2):
                    link(nc.vector.bn_stats(stats[:, t, 6 * j:6 * j + 6], xn[:, t, 512 * j:512 * j + 512]))
                link(nc.vector.bn_aggr(mv[:, t, :], stats[:, t, :]))

            def ln_apply(which, ready):
                nc.vector.tensor_scalar(veps, mv[:, :, 1], EPS, None, ALU.add).then_inc(var_done, 1)
                dve.wait_ge(std_done, which + 1)
                link(nc.vector.reciprocal(rstd, std))
                dve.wait_ge(gain_in[which], 32)
                for t in range(NT):
                    r = xn[:, t, :]
                    link(nc.vector.tensor_scalar(r, r, mv[:, t, 0:1], rstd[:, t:t + 1], ALU.subtract, ALU.mult))
                    link(nc.vector.tensor_tensor(r, r, g_row, ALU.mult))
                    nc.vector.tensor_tensor(r, r, b_row, ALU.add).then_inc(ready, 1)

            for t in range(NT):
                dve.wait_ge(x_in[t], 16)
                ln_stats(t)
            ln_apply(0, ln_in_done)
            dve.wait_ge(lam_in, 80)
            for a in range(2):
                link(nc.vector.tensor_tensor_reduce(lam4[:, 2 * a, :], lam4[:, 2 * a, :], lam4[:, 2 * a + 1, :],
                                                    1.0, 0.0, ALU.mult, ALU.add, lam2[:, a:a + 1]))
            nc.vector.tensor_scalar(lam2, lam2, 0.0, None, ALU.add).then_inc(lam_dots, 1)
            dve.wait_ge(lam_exp, 1)
            link(nc.vector.tensor_scalar(nlam, elam[:, 1:2], elam[:, 0:1], -LAMBDA_INIT, ALU.subtract, ALU.add))
            link(nc.vector.tensor_scalar(sub_g, sub_g, OUT_SCALE, None, ALU.mult))

            dve.wait_ge(iota_done, 1)
            link(nc.vector.tensor_scalar(bias_h, dist, -1.0, None, ALU.mult))
            link(nc.vector.tensor_tensor(dist, dist, bias_h, ALU.max))
            u = 0

            def take_output(v, h, tq):
                dve.wait_ge(pv_mm, v + 1)
                o = vf[:, tq, 512 + h * P:512 + (h + 1) * P]
                nc.vector.tensor_copy(o, bank(2 + v % 2)[:, 0:P]).then_inc(o_ev, 1)

            units = [(h, t0, nt, qt) for h in range(H) for t0, nt in BATCHES for qt in range(nt)]
            for u, (h, t0, nt, qt) in enumerate(units):
                if u % NT == 0:
                    link(nc.vector.tensor_scalar(bias_h, dist, -SLOPES[h], None, ALU.mult))
                w = nt * P
                first = S_SAMPLE - P - qt * P
                for c in range(2):
                    dve.wait_ge(s_mm, 2 * u + c + 1)
                    link(nc.vector.tensor_tensor_reduce(prob[:, c, 0:w], wide[c][:, 0:w], bias_h[:, first:first + w],
                                                        1.0, -3.0e38, ALU.add, ALU.max, rmax[:, c:c + 1]))
                    nc.vector.tensor_scalar(nrmax[:, c:c + 1], rmax[:, c:c + 1], -1.0, None, ALU.mult)\
                        .then_inc(biased, 1)
                if u >= 1:
                    hh, tt0, _, qq = units[u - 1]
                    take_output(u - 1, hh, tt0 + qq)
                dve.wait_ge(exped, 2 * u + 2)
                link(nc.vector.reciprocal(rinv, psum_row))
                link(nc.vector.tensor_scalar(rinv[:, 1:2], rinv[:, 1:2], nlam, None, ALU.mult))
                if u:
                    dve.wait_ge(at_mm, att_groups(u, 0))
                link(nc.vector.tensor_scalar(diff[:, 0:w], prob[:, 0, 0:w], rinv[:, 0:1], None, ALU.mult))
                nc.vector.scalar_tensor_tensor(out=diff[:, 0:w], in0=prob[:, 1, 0:w], scalar=rinv[:, 1:2],
                                               in1=diff[:, 0:w], op0=ALU.mult, op1=ALU.add).then_inc(diffed, 1)
                dve.wait_ge(diffed, u + 1)
            hh, tt0, _, qq = units[-1]
            take_output(len(units) - 1, hh, tt0 + qq)
            dve.wait_ge(o_ev, len(units))
            for t in range(NT):
                for h in range(H):
                    o = vf[:, t, 512 + h * P:512 + (h + 1) * P]
                    last = nc.vector.tensor_tensor_reduce(scratch, o, o, 1.0 / P, EPS, ALU.mult, ALU.add,
                                                          ssq[:, t * H + h:t * H + h + 1])
                    link(last)
            nc.vector.tensor_scalar(ssq, ssq, 0.0, None, ALU.add).then_inc(ssq_done, 1)
            dve.wait_ge(rms_done, 1)
            link(nc.vector.reciprocal(rrms, rms))
            for t in range(NT):
                for h in range(H):
                    o = vf[:, t, 512 + h * P:512 + (h + 1) * P]
                    last = nc.vector.scalar_tensor_tensor(out=o, in0=o, scalar=rrms[:, t * H + h:t * H + h + 1],
                                                          in1=sub_g, op0=ALU.mult, op1=ALU.mult)
                    if h < H - 1:
                        link(last)
                last.then_inc(o_norm, 1)
            for n in range(2 * NT):
                t, half = divmod(n, 2)
                dve.wait_ge(wo_mm, n + 1)
                r = xn[:, t, 512 * half:512 * half + 512]
                nc.vector.scalar_tensor_tensor(out=r, in0=r, scalar=ALPHA, in1=bank(n % 8),
                                               op0=ALU.mult, op1=ALU.add).then_inc(wo_add, 1)
                dve.wait_ge(wo_add, n + 1)
                if half:
                    ln_stats(t)
            ln_apply(1, x1_done)

            steps = [0]

            def step(ins):
                steps[0] += 1
                ins.then_inc(chain, 1)
                dve.wait_ge(chain, steps[0])

            def restart():
                dve.wait_ge(chain, steps[0])
                dve.sem_clear(chain)
                steps[0] = 0

            def retrieval(t, gathers):
                def begin():
                    dve.wait_ge(sc_cur, t + 1)
                    dve.sem_inc(scores_seen, 1)

                def top16(v, i, row):
                    for k in range(2):
                        v8 = v[:, 8 * k:8 * k + 8]
                        step(nc.vector.max(v8, row))
                        step(nc.vector.max_index(i[:, 8 * k:8 * k + 8], v8, row))
                        if k == 0:
                                step(nc.vector.match_replace(row, v8, row, NEG))

                def rows(r):
                    if r == 0:
                        begin()
                    top16(vals[:, r, :], iu[:, r, :], scur[:, r, :])

                def sums():
                    nc.vector.tensor_copy(idf, iu.rearrange("p r k -> p (r k)")).then_inc(sc_used, 1)
                    dve.wait_ge(sc_used, t + 1)
                    c4 = cand.rearrange("p (h a b) -> p h a b", h=PH, a=TOPK)
                    shape = [P, PH, TOPK, TOPK]
                    step(nc.vector.tensor_tensor(c4, vals[:, 0:PH, :].unsqueeze(3).broadcast_to(shape),
                                                 vals[:, PH:2 * PH, :].unsqueeze(2).broadcast_to(shape), ALU.add))

                def heads(h):
                    c = cand.rearrange("p (h n) -> p h n", h=PH)[:, h, :]
                    top16(best[:, h, :], posu[:, h, :], c)

                def positions():
                    flat = posu.rearrange("p h k -> p (h k)")
                    step(nc.vector.tensor_scalar(pshift, flat, 4, None, ALU.logical_shift_right))
                    step(nc.vector.tensor_copy(pabf[:, 0, :], pshift))
                    step(nc.vector.tensor_scalar(pshift, flat, TOPK - 1, None, ALU.bitwise_and))
                    step(nc.vector.tensor_copy(pabf[:, 1, :], pshift))

                def lookup(c, part):
                    p3 = pick.rearrange("p (s a) -> p s a", a=TOPK)
                    if part == 0:
                        step(nc.vector.tensor_tensor(
                            p3, pabf[:, c, :].unsqueeze(2).broadcast_to([P, NSLOT, TOPK]),
                            iota16.unsqueeze(1).broadcast_to([P, NSLOT, TOPK]), ALU.is_equal))
                    elif part == 1:
                        shape = [P, PH, TOPK, TOPK]
                        p4 = pick.rearrange("p (h k a) -> p h k a", h=PH, k=TOPK)
                        rows = idf.rearrange("p (r k) -> p r k", r=2 * PH)[:, c * PH:(c + 1) * PH, :]
                        step(nc.vector.tensor_tensor(p4, p4, rows.unsqueeze(2).broadcast_to(shape), ALU.mult))
                    else:
                        step(nc.vector.tensor_reduce(iab[:, c, :], p3, AX.X, ALU.add))

                def indices():
                    if gathers:
                        step(nc.vector.scalar_tensor_tensor(out=eidf, in0=iab[:, 0, :], scalar=float(NK),
                                                            in1=iab[:, 1, :], op0=ALU.mult, op1=ALU.add))
                        step(nc.vector.tensor_copy(idx[:, bass.ds(t, 1), :].rearrange("p a s -> p (a s)"), eidf))

                def gates_a():
                    step(nc.vector.tensor_copy(mx8, best[:, :, 0]))
                    nc.vector.tensor_tensor(best, best, mx8.unsqueeze(2).broadcast_to([P, PH, TOPK]),
                                            ALU.subtract).then_inc(best_sub, 1)

                def gates_b():
                    dve.wait_ge(gate_exp, t + 1)
                    step(nc.vector.tensor_reduce(gsum, best, AX.X, ALU.add))
                    step(nc.vector.reciprocal(gsum, gsum))
                    dst = gates_g[:, bass.ds(t, 1), :].rearrange("p a s -> p (a s)") if gathers else gate
                    nc.vector.tensor_tensor(dst.rearrange("p (h k) -> p h k", h=PH), best,
                                            gsum.unsqueeze(2).broadcast_to([P, PH, TOPK]), ALU.mult)\
                        .then_inc(retrieved, 1)

                out_p = [lambda r=r: rows(r) for r in range(2 * PH)] + [sums]
                out_p += [lambda h=h: heads(h) for h in range(PH)] + [positions]
                out_p += [lambda c=c, k=k: lookup(c, k) for c in range(2) for k in range(3)]
                return out_p + [indices, gates_a, gates_b]

            dve.wait_ge(iota_done, 3)
            with dve.Fori(0, NG) as t:
                for piece in retrieval(t, True):
                    piece()
                restart()
            for piece in retrieval(NG, False):
                piece()
            restart()

            def hot_rows(i, b):
                dve.wait_ge(g_mm, i * NB + b + 1)
                for k in range(GB_T):
                    t = GB_T * b + k
                    last = nc.vector.tensor_scalar(hot[:, 0, 4 * (b % 2) + k, :], iota_row, slot_t[:, 0, t:t + 1],
                                                   slot_t[:, 2, t:t + 1], ALU.is_equal, ALU.mult)
                last.then_inc(hot_i, 1)

            with dve.Fori(0, ND - 1) as i:
                dve.wait_ge(turn_ev, i + 1)
                pieces = retrieval(i + (NG + 1), False)
                for k in range(max(NB, len(pieces))):
                    if k < len(pieces):
                        pieces[k]()
                    if k < NB:
                        hot_rows(i, k)
                restart()
            dve.wait_ge(turn_ev, ND)
            for b in range(NB):
                hot_rows(ND - 1, b)

            for n in range(2 * ND):
                t, half = divmod(n, 2)
                cols = slice(t * P, (t + 1) * P)
                rows = slice(4 * half, 4 * half + 4)
                dve.wait_ge(xh_ev, n + 1)
                nc.vector.tensor_tensor(xl[:, rows, cols], bank(n % 8).rearrange("p (c t) -> p c t", c=4),
                                        xh[:, rows, cols].bitcast(F32), ALU.subtract).then_inc(xl_ev, 1)
            dve.wait_ge(xl_ev, 2 * ND)
            for t in range(ND):
                nc.vector.tensor_scalar(xn[:, NG + t, :], xn[:, NG + t, :], ALPHA, None, ALU.mult)\
                    .then_inc(y_add, 1)
            dve.sem_inc(gated, 2)
            dve.sem_inc(al_done, 2)
            dve.sem_inc(started, 1)

            def tile(g, first, last):
                y = xn[:, bass.ds(g, 1), :].rearrange("p a n -> p (a n)")

                def slot(s):
                    k, (v, c) = s % RING, divmod(s, NSLOT)
                    dve.wait_ge(row_in[k], use(g, c, v) * 16)
                    if v == 0:
                        nc.vector.tensor_tensor_reduce(ring[:, k, :], ring[:, k, :], xcur, 1.0, 0.0, ALU.mult, ALU.add,
                                                       act[:, c:c + 1]).then_inc(row_used[k], 1)
                    else:
                        if c:
                            dve.wait_ge(row_used[(c - 1) % RING], use(g, c - 1, 1) + 1)
                        nc.vector.scalar_tensor_tensor(out=y, in0=ring[:, k, :], scalar=coef[:, c:c + 1], in1=y,
                                                       op0=ALU.mult, op1=ALU.add).then_inc(row_used[k], 1)

                def coefficients():
                    for k in range(RING):
                        dve.wait_ge(row_used[k], use(g, NSLOT - RING + k, 0) + 1)
                    dve.sem_inc(acts, 1)
                    dve.wait_ge(gacts, g + 1)
                    nc.vector.tensor_tensor(coef, gact, gates_g[:, bass.ds(g, 1), :].rearrange("p a s -> p (a s)"),
                                            ALU.mult).then_inc(coefs, 1)
                    nc.vector.tensor_scalar(y, xcur, ALPHA, None, ALU.mult).then_inc(coefs, 1)
                    dve.wait_ge(coefs, g * 2 + 2)

                def gated_part(q, e):
                    dve.wait_ge(hid_done, q * 2 + e + 3)
                    dve.wait_ge(g_in[e], q * 16 + 16)
                    nc.vector.tensor_tensor(hid[:, e, :], hid[:, e, :], g_in_sb[:, e, :], ALU.mult).then_inc(gated, 1)

                def lo_part(q, par, e):
                    dve.wait_ge(ah_done, q * 2 + e + 1)
                    nc.vector.tensor_tensor(al[:, par, e, :], hid[:, e, :], ah[:, par, e, :].bitcast(F32),
                                            ALU.subtract).then_inc(al_done, 1)

                dve.wait_ge(x_cur, g + 1)
                for k in range(KP):
                    q, par = g * KP + k, k % 2
                    s = [k * SP_]

                    def slots(n):
                        for _ in range(n):
                            slot(s[0])
                            s[0] += 1

                    if k == KP // 2:
                        coefficients()
                    adds = not (first and k == 0)
                    slots(6)
                    gated_part(q, 0)
                    slots(1)
                    gated_part(q, 1)
                    slots(1)
                    for t in range(ND):
                        if adds:
                            add(q, t)
                        if t < 2:
                            lo_part(q, par, t)
                        slots(SP_ // 2 * (t + 1) // ND - SP_ // 2 * t // ND)
                    assert s[0] == (k + 1) * SP_

            def add(q, t):
                n = q * ND + (t - ND)
                dve.wait_ge(y_mm, n + (2 * ND + 1))
                dve.wait_ge(y_add, n + 1)
                nc.vector.tensor_tensor(xn[:, NG + t, :], xn[:, NG + t, :], wide[t % 2][:, :], ALU.add)\
                    .then_inc(y_add, 1)

            tile(0, True, False)
            with dve.Fori(1, NG - 1) as g:
                tile(g, False, False)
            tile(NG - 1, False, True)
            for t in range(ND):
                add(NP, t)
            dve.wait_ge(y_add, ND * NP + ND)
            for k in range(RING):
                dve.wait_ge(row_used[k], use(NG - 1, NSLOT - RING + k, 1) + 1)
            for t in range(NT):
                ln_stats(t)
            ln_apply(2, y_done)


def dft_tables(n, scale):
    a = 2.0 * np.pi * ((np.arange(n)[:, None] * np.arange(n)[None, :]) % n) / n
    return np.cos(a) * scale, np.sin(a) * scale


def kernel(**inputs):
    import numpy as _np
    import concourse.bacc as _bacc
    from concourse.bass_utils import run_bass_kernel_spmd as _run

    f = {k: _np.asarray(v) for k, v in inputs.items()}
    c, s = dft_tables(P, 1.0)
    arrays = {
        "x": _np.concatenate([f["x_prompt"][0], f["x_sample"][0]], axis=0),
        "ln_g": f["ln_in_g"], "ln_b": f["ln_in_b"], "w_in": f["w_in"][0],
        "lq1": f["lambda_q1"][0], "lk1": f["lambda_k1"][0], "lq2": f["lambda_q2"][0], "lk2": f["lambda_k2"][0],
        "subln_g": f["subln_g"][0], "w_f": f["w_fourier"][0], "b_f": f["b_fourier"][0], "w_out": f["w_out"][0],
        "ln1_g": f["ln1_g"][0], "ln1_b": f["ln1_b"][0], "wq": f["peer_wq"][0],
        "skt": _np.ascontiguousarray(f["peer_subkeys"][0].transpose(1, 3, 0, 2)).reshape(2, DQK, PH, NK),
        "pu": f["peer_u"][0],
        "ut": f["peer_u"][0].reshape(P, NK, DC, P).transpose(1, 3, 2, 0).reshape(NK, P, D),
        "pv": f["peer_v"][0], "ln2_g": f["ln2_g"][0], "ln2_b": f["ln2_b"][0],
        "dft_sample": _np.stack(dft_tables(S_SAMPLE, (S_SAMPLE * P) ** -0.5)).astype(_np.float32),
        "dft_prompt": _np.stack(dft_tables(S_PROMPT, (S_PROMPT * P) ** -0.5)).astype(_np.float32),
        "dft_chan": _np.stack([c, -s]).astype(_np.float32),
    }
    nc = _bacc.Bacc("TRN2", target_bir_lowering=False, num_devices=1)
    args, feed = [], {}
    for name, a in arrays.items():
        feed[f"in_{name}"] = _np.ascontiguousarray(a)
        args.append(nc.dram_tensor(f"in_{name}", a.shape, F32, kind="ExternalInput").ap())
    args.append(nc.dram_tensor("spread_gates", (NK, P, TD), F32, kind="Internal").ap())
    args.append(nc.dram_tensor("out_y", (T, D), F32, kind="ExternalOutput").ap())
    build(nc, *args)
    r = _run(nc, [feed], core_ids=[0])
    y = r.results[0]["out_y"]
    return y[None, :S_PROMPT], y[None, S_PROMPT:]
```

```python
from contextlib import ExitStack

import numpy as np

import concourse.bass as bass
from concourse import mybir

F32 = mybir.dt.float32
U32 = mybir.dt.uint32
F32R = mybir.dt.float32r
BF16 = mybir.dt.bfloat16
ALU = mybir.AluOpType
ACT = mybir.ActivationFunctionType
AX = mybir.AxisListType

P = 128
D = 1024
DC = D // P
S_PROMPT, S_SAMPLE = 256, 1024
NT = (S_PROMPT + S_SAMPLE) // P
T = NT * P
H = 4
HF = 4
DQK = 64
PH = 8
NK = 128
TOPK = 16
NSLOT = PH * TOPK
EPS = 1e-5
ALPHA = 2.0 ** 0.25
LAMBDA_INIT = 0.8 - 0.6
OUT_SCALE = 1.0 - LAMBDA_INIT
SLOPES = [2.0 ** (-8.0 * (h + 1) / H) for h in range(H)]
BATCHES = [(2, S_SAMPLE // P), (0, S_PROMPT // P)]
DIST_W = 2 * S_SAMPLE - P
RING = 8
NG = 4
ND = NT - NG
TD = ND * P
HN = TD // 2
NP = NK // 2
KP = NP // NG
SP_ = 2 * NSLOT // KP
GB_T = 4
NB = P // GB_T
LOAD_AT, EXP_AT = 18, 26
HOT_G = 2
assert KP * NG == NP and SP_ * KP == 2 * NSLOT and 2 * HN == TD and SP_ % RING == 0
NEG = -3.0e38
POOL_ORDER = "6 v0 2 v1 2 u0 3 u1 3"
DVE_ORDER = "5 g0 5 l0 a 1 g1 a 1 a l1 1 a 1 a 1 a 1"


def token_blocks():
    return [(a, min(a + 512, T)) for a in range(0, T, 512)]


def build(nc, x, ln_g, ln_b, w_in, lq1, lk1, lq2, lk2, subln_g, w_f, b_f, w_out, ln1_g, ln1_b,
          wq, skt, pu, ut, pv, ln2_g, ln2_b, dft_sample, dft_prompt, dft_chan, gates, out):
    ctx = ExitStack()
    with ctx:
        origin = (nc.sbuf_base + 31) // 32 * 32

        def sb(name, at, cols, dt=F32):
            assert origin + 4 * (at + cols) <= nc.sbuf_usable_end
            return nc.alloc_sbuf_tensor_at(name, [P, cols], dt, offset=origin + 4 * at)

        def sem(name):
            return ctx.enter_context(nc.semaphore(name))

        BIG, XLN, QK, WB, GB, SM = 0, 20480, 30720, 40960, 49152, 51200
        big = sb("big", BIG, NT * 2 * D)
        xln = sb("xln", XLN, NT * D)
        qk = sb("qk", QK, DC * T)
        wbuf = sb("wbuf", WB, 8 * D)
        gb = sb("gb", GB, 2 * D)
        ident = sb("ident", SM, P)
        idx_sb = sb("idx_sb", SM + P, (NG + 1) * P, U32)
        small = sb("small", SM + (NG + 2) * P, 1200)
        ah_sb, al_sb = sb("ah_sb", BIG, 4 * TD, F32R), sb("al_sb", BIG + 4 * TD, 4 * TD, F32R)
        peer_sb = sb("peer_sb", BIG + 8 * TD, 2 * D)
        x_at = BIG + 8 * TD + 2 * D
        xh_sb, xl_sb = sb("xh_sb", x_at, DC * TD, F32R), sb("xl_sb", x_at + DC * TD, DC * TD, F32R)
        assert x_at >= BIG + 8 * D and x_at + 2 * DC * TD <= XLN
        uh_sb, ul_sb = sb("uh_sb", QK, 2 * D, F32R), sb("ul_sb", QK + 2 * D, 2 * D, F32R)
        vh_sb, vl_sb = sb("vh_sb", QK + 4 * D, 2 * D, F32R), sb("vl_sb", QK + 6 * D, 2 * D, F32R)
        gate_sb = sb("gate_sb", QK + 8 * D, 2 * D)

        xt = big[:, 0:DC * T].rearrange("p (c t) -> p c t", c=DC)
        vf = big[:, DC * T:].rearrange("p (t n) -> p t n", t=NT)
        sc = big[:, :].rearrange("p (t r) -> p t r", t=NT)
        xn = xln[:, :].rearrange("p (t n) -> p t n", t=NT)
        qkv = qk[:, :].rearrange("p (c t) -> p c t", c=DC)
        w8 = wbuf[:, :].rearrange("p (m c n) -> p m c n", m=8, c=DC)
        w2 = wbuf[:, :].rearrange("p (m c n) -> p m c n", m=2, c=DC)
        wfull = wbuf[:, :].rearrange("p (c n) -> p c n", c=DC)
        g_row, b_row = gb[:, 0:D], gb[:, D:2 * D]
        cc, scn = gb[:, 0:P], gb[:, P:2 * P]
        wf = gb[:, 2 * P:2 * P + HF * P].rearrange("p (g e) -> p g e", g=HF)
        bf = gb[:, 6 * P:6 * P + HF]
        trig = big[:, 0:4096].rearrange("p (k g s) -> p k g s", k=2, g=HF)
        zt = big[:, 4096:5120].rearrange("p (b s) -> p b s", b=2)
        dist = wbuf[:, 0:DIST_W]
        bias_h = wbuf[:, DIST_W:2 * DIST_W]
        o0 = 2 * DIST_W
        prob = wbuf[:, o0:o0 + 2 * D].rearrange("p (c k) -> p c k", c=2)
        diff = wbuf[:, o0 + 2 * D:o0 + 3 * D]
        difft = wbuf[:, o0 + 3 * D:o0 + 4 * D].rearrange("p (k q) -> p k q", k=8)
        assert o0 + 4 * D <= 8 * D
        sk = gb[:, 0:PH * NK].rearrange("p (h n) -> p h n", h=PH)

        n_small = [0]

        def sm(cols):
            a = n_small[0]
            n_small[0] += cols
            assert n_small[0] <= 1200
            return small[:, a:a + cols]

        stats = sm(NT * 12).rearrange("p (t s) -> p t s", t=NT)
        mv = sm(NT * 2).rearrange("p (t s) -> p t s", t=NT)
        veps = sm(NT)
        std = sm(NT)
        rstd = sm(NT)
        scratch = sm(P)
        gate = sm(NSLOT)
        iota_row = sm(P)
        n_mark = n_small[0]
        lam4 = sm(4 * DQK).rearrange("p (a d) -> p a d", a=4)
        sub_g = sm(P)
        lam2, elam, nlam = sm(2), sm(2), sm(1)
        rmax = sm(2)
        nrmax = sm(2)
        psum_row = sm(2)
        rinv = sm(2)
        ssq = sm(NT * H)
        rms = sm(NT * H)
        rrms = sm(NT * H)
        n_small[0] = n_mark
        iota16 = sm(TOPK // 2).bitcast(BF16)
        mx8 = sm(PH)
        best = sm(NSLOT).rearrange("p (h k) -> p h k", h=PH)
        gsum = sm(PH)

        at = [0]

        def wk(cols):
            a = at[0]
            at[0] += cols
            assert at[0] <= DC * T
            return qk[:, a:a + cols]

        scur = wk(2 * PH * NK).rearrange("p (r n) -> p r n", r=2 * PH)
        cand = wk(PH * TOPK * TOPK)
        pick = wk(NSLOT * TOPK // 2).bitcast(BF16)
        vals = wk(2 * PH * TOPK).rearrange("p (r k) -> p r k", r=2 * PH)
        idf = wk(PH * TOPK).bitcast(BF16)
        pabf = wk(NSLOT).bitcast(BF16).rearrange("p (c s) -> p c s", c=2)
        iab = wk(2 * NSLOT).rearrange("p (c s) -> p c s", c=2)
        eidf = wk(NSLOT)
        posu = wk(NSLOT).bitcast(U32).rearrange("p (h k) -> p h k", h=PH)
        pshift = wk(NSLOT).bitcast(U32)
        iu = wk(2 * PH * TOPK).bitcast(U32).rearrange("p (r k) -> p r k", r=2 * PH)
        hot = wk(16 * P).rearrange("p (w b n) -> p w b n", w=2, b=8)
        slot_t = wk(3 * P).rearrange("p (w t) -> p w t", w=3)
        idx = idx_sb[:, 0:NG * P].rearrange("p (t s) -> p t s", t=NG)
        idx_u = idx_sb[:, NG * P:]
        spread = [wbuf[:, :].rearrange("p (j t) -> p j t", j=NK), big[:, 0:8 * D].rearrange("p (j t) -> p j t", j=NK)]
        xh = xh_sb[:, :].rearrange("p (c t) -> p c t", c=DC)
        xl = xl_sb[:, :].rearrange("p (c t) -> p c t", c=DC)
        ah = ah_sb[:, :].rearrange("p (b e t) -> p b e t", b=2, e=2)
        al = al_sb[:, :].rearrange("p (b e t) -> p b e t", b=2, e=2)
        uh = uh_sb[:, :].rearrange("p (e c i) -> p e c i", e=2, c=DC)
        ul = ul_sb[:, :].rearrange("p (e c i) -> p e c i", e=2, c=DC)
        vh = vh_sb[:, :].rearrange("p (e d) -> p e d", e=2)
        vl = vl_sb[:, :].rearrange("p (e d) -> p e d", e=2)
        g_in_sb, hid = gate_sb[:, 0:TD], gate_sb[:, TD:2 * TD]
        act, coef, gact = (gate_sb[:, 2 * TD + k * NSLOT:2 * TD + (k + 1) * NSLOT] for k in range(3))
        assert 2 * TD + 3 * NSLOT <= 2 * D
        raw = wbuf[:, 0:2 * D].rearrange("p (e n) -> p e n", e=2)
        ring = [wbuf[:, k * D:(k + 1) * D] for k in range(2, 8)] + [peer_sb[:, 0:D], gb[:, 0:D]]
        assert len(ring) == RING
        xcur = peer_sb[:, D:2 * D]
        gates_g = gb[:, D:D + NG * NSLOT].rearrange("p (t s) -> p t s", t=NG)
        idx_v = gb[:, D + NG * NSLOT:D + (NG + 1) * NSLOT].bitcast(U32)
        assert (NG + 1) * NSLOT <= D

        twin = [ctx.enter_context(nc.psum_tensor(f"twin{b}", [P, 1024], F32)) for b in range(4)]
        wide = twin[2:]
        act_psum = [t[:, :].rearrange("p (h n) -> p h n", h=2) for t in twin[:2]]

        def bank(n):
            return twin[n // 2][:, 512 * (n % 2):512 * (n % 2) + 512]

        x_in = [sem(f"x_in{t}") for t in range(NT)]
        gain_in = [sem(f"gain_in{k}") for k in range(3)]
        w_qk_in = [sem(f"w_qk_in{m}") for m in range(8)]
        w_vf_in = [sem(f"w_vf_in{m}") for m in range(2)]
        dft_in = [sem(f"dft_in{k}") for k in range(2)]
        four_in = sem("four_in")
        lam_in = sem("lam_in")
        w_out_in = sem("w_out_in")
        wq_in = [sem(f"wq_in{m}") for m in range(8)]
        sk_in = sem("sk_in")
        const_done = sem("const_done")
        dve_chain = sem("dve_chain")
        var_done = sem("var_done")
        std_done = sem("std_done")
        ln_in_done = sem("ln_in_done")
        xt_mm, xt_ev = sem("xt_mm"), sem("xt_ev")
        qk_mm, qk_ev = sem("qk_mm"), sem("qk_ev")
        vf_mm, vf_ev = sem("vf_mm"), sem("vf_ev")
        dft_mm, dft_ev = sem("dft_mm"), sem("dft_ev")
        z_mm, z_ev = sem("z_mm"), sem("z_ev")
        f_mm, f_ev = sem("f_mm"), sem("f_ev")
        lam_dots, lam_exp = sem("lam_dots"), sem("lam_exp")
        s_mm, biased, exped, diffed = sem("s_mm"), sem("biased"), sem("exped"), sem("diffed")
        at_mm, at_ev, pv_mm, o_ev = sem("at_mm"), sem("at_ev"), sem("pv_mm"), sem("o_ev")
        ssq_done, rms_done, o_norm = sem("ssq_done"), sem("rms_done"), sem("o_norm")
        ot_mm, ot_ev = sem("ot_mm"), sem("ot_ev")
        wo_mm, wo_add = sem("wo_mm"), sem("wo_add")
        x1_done = sem("x1_done")
        x1t_mm, x1t_ev = sem("x1t_mm"), sem("x1t_ev")
        wq_mm, wq_ev = sem("wq_mm"), sem("wq_ev")
        sc_mm, sc_ev = sem("sc_mm"), sem("sc_ev")
        iota_done = sem("iota_done")
        sc_cur = sem("sc_cur")
        chain = sem("chain")
        scores_seen, slots_free = sem("scores_seen"), sem("slots_free")
        sc_used, best_sub, gate_exp = sem("sc_used"), sem("best_sub"), sem("gate_exp")
        retrieved = sem("retrieved")
        turn_mm, turn_ev = sem("turn_mm"), sem("turn_ev")
        hot_g, hot_v, hot_j = sem("hot_g"), sem("hot_v"), sem("hot_j")
        hot_dist = sem("hot_dist")
        g_mm, g_ev = sem("g_mm"), sem("g_ev")
        g_out = [sem(f"g_out{m}") for m in range(2)]
        xh_mm, xh_ev, xl_ev = sem("xh_mm"), sem("xh_ev"), sem("xl_ev")
        u_in = [sem(f"u_in{e}") for e in range(2)]
        v_in = [sem(f"v_in{e}") for e in range(2)]
        g_in = sem("g_in")
        uh_done, ul_done = sem("uh_done"), sem("ul_done")
        vh_done, vl_done = sem("vh_done"), sem("vl_done")
        h_mm, hid_done = sem("h_mm"), sem("hid_done")
        gated, ah_done, al_done = sem("gated"), sem("ah_done"), sem("al_done")
        y_mm, y_add = sem("y_mm"), sem("y_add")
        started = sem("started")
        x_cur, idx_copied = sem("x_cur"), sem("idx_copied")
        acts, gacts, coefs = sem("acts"), sem("gacts"), sem("coefs")
        row_in = [sem(f"row_in{k}") for k in range(RING)]
        row_used = [sem(f"row_used{k}") for k in range(RING)]
        y_done, y_out = sem("y_done"), sem("y_out")

        block = ctx.enter_context(nc.Block())

        USES = 2 * NSLOT // RING

        def use(t, s, v):
            return t * USES + (v * NSLOT + s) // RING + 1

        @block.sync
        def _(sp):
            for t in range(NT):
                sp.dma_start(xn[:, t, :], x[t * P:(t + 1) * P, :]).then_inc(x_in[t], 16)
                if t == 1:
                    sp.dma_start(g_row, ln_g.partition_broadcast(P)).then_inc(gain_in[0], 16)
                    sp.dma_start(b_row, ln_b.partition_broadcast(P)).then_inc(gain_in[0], 16)
            w_in_v = w_in.rearrange("(c p) n -> p c n", p=P)
            for m in range(8):
                sp.dma_start(w8[:, m], w_in_v[:, :, m * P:(m + 1) * P]).then_inc(w_qk_in[m], 16)
            for a, v in enumerate((lq1, lk1, lq2, lk2)):
                sp.dma_start(lam4[:, a, :], v.partition_broadcast(P)).then_inc(lam_in, 16)
            sp.dma_start(sub_g, subln_g.partition_broadcast(P)).then_inc(lam_in, 16)
            blocks = len(token_blocks())
            for m in range(2):
                sp.wait_ge(qk_mm, 4 * (m + 1) * blocks)
                sp.dma_start(w2[:, m], w_in_v[:, :, D + 512 * m:D + 512 * (m + 1)]).then_inc(w_vf_in[m], 16)
            sp.wait_ge(ln_in_done, NT)
            sp.dma_start(cc, dft_chan[0]).then_inc(four_in, 16)
            sp.dma_start(scn, dft_chan[1]).then_inc(four_in, 16)
            sp.dma_start(wf, w_f.rearrange("g c e -> c g e")).then_inc(four_in, 16)
            sp.dma_start(bf, b_f.rearrange("g e -> e g"), allow_slow_non_contiguous=True).then_inc(four_in, 16)
            for n in range(3):
                for k in range(2):
                    if n == 0:
                        sp.wait_ge(vf_mm, NT * (k + 1))
                    else:
                        sp.wait_ge(dft_mm, 2 * HF * (n - 1) + HF * (k + 1))
                    if n < 2:
                        sp.dma_start(w2[:, k], dft_sample[k].rearrange("(c p) s -> p c s", p=P)[
                            :, :, 512 * n:512 * n + 512]).then_inc(dft_in[k], 16)
                    else:
                        sp.dma_start(w2[:, k, 0:2, 0:S_PROMPT],
                                     dft_prompt[k].rearrange("(c p) s -> p c s", p=P)).then_inc(dft_in[k], 16)
            sp.wait_ge(f_mm, 3 * HF)
            sp.wait_ge(f_ev, 3 * HF)
            sp.dma_start(g_row, ln1_g.partition_broadcast(P)).then_inc(gain_in[1], 16)
            sp.dma_start(b_row, ln1_b.partition_broadcast(P)).then_inc(gain_in[1], 16)
            sp.wait_ge(pv_mm, NT * H)
            sp.wait_ge(diffed, NT * H)
            sp.dma_start(wfull, w_out.rearrange("(c p) n -> p c n", p=P)).then_inc(w_out_in, 16)
            sp.wait_ge(wo_mm, 2 * NT)
            wq_v = wq.rearrange("(c p) n -> p c n", p=P)
            for m in range(8):
                sp.dma_start(w8[:, m], wq_v[:, :, m * P:(m + 1) * P]).then_inc(wq_in[m], 16)
            sp.wait_ge(x1_done, NT)
            sp.dma_start(sk, skt.rearrange("c d h n -> (c d) h n")).then_inc(sk_in, 16)
            sp.wait_ge(sc_mm, 4 * NT)
            g_by_i = gates.rearrange("j i t -> i j t")
            for m in range(2):
                sp.sem_inc(g_out[m], 16)

            def store_gates(i, m):
                sp.wait_ge(g_ev, i * NB + (NB // 2 * (m + 1) + 4))
                sp.dma_start(g_by_i[:, :, bass.ds(i * P + 64 * m, 64)], spread[m]).then_inc(g_out[m], 16)

            with sp.Fori(0, ND - 1) as i:
                for m in range(2):
                    store_gates(i, m)
            store_gates(ND - 1, 0)
            v_by_j = pv.rearrange("(i j) d -> j i d", j=NK)

            def load_u(c, e):
                sp.dma_start(raw[:, e, :], ut[bass.ds(c, 1), :, :].rearrange("a p n -> (a p) n"))\
                    .then_inc(u_in[e], 16)

            def load_gates(c):
                sp.wait_ge(gated, c + 1)
                sp.dma_start(g_in_sb, gates[bass.ds(c, 1), :, :].rearrange("a p n -> (a p) n")).then_inc(g_in, 16)

            def load_v(c, e):
                sp.dma_start(raw[:, e, :], v_by_j[bass.ds(c, 1), :, :].rearrange("a p n -> (a p) n"))\
                    .then_inc(v_in[e], 16)

            sp.wait_ge(g_out[0], 16 * (ND + 1))
            for e in range(2):
                load_u(e, e)
            store_gates(ND - 1, 1)
            sp.wait_ge(g_out[1], 16 * (ND + 1))
            with sp.Fori(0, NP - 1) as q:
                load_gates(q * 2)
                for e in range(2):
                    sp.wait_ge(ul_done, q * 2 + e + 2)
                    sp.wait_ge(vl_done, q * 2 + e + 1)
                    load_u(q * 2 + (e + 2), e)
                load_gates(q * 2 + 1)
                for e in range(2):
                    sp.wait_ge(ul_done, q * 2 + e + 4)
                    load_v(q * 2 + e, e)
            load_gates(2 * NP - 2)
            load_gates(2 * NP - 1)
            for e in range(2):
                sp.wait_ge(vl_done, 2 * (NP - 1) + e + 1)
                load_v(2 * (NP - 1) + e, e)
            sp.wait_ge(y_add, ND * NP + ND)
            sp.wait_ge(gated, 2 * NP + 1)
            sp.wait_ge(coefs, 2 * NG)
            sp.wait_ge(al_done, 2 * NP + 2)
            sp.dma_start(g_row, ln2_g.partition_broadcast(P)).then_inc(gain_in[2], 16)
            sp.dma_start(b_row, ln2_b.partition_broadcast(P)).then_inc(gain_in[2], 16)
            for t in range(NT):
                sp.wait_ge(y_done, t + 1)
                sp.dma_start(out[t * P:(t + 1) * P, :], xn[:, t, :]).then_inc(y_out, 16)
            sp.wait_ge(y_out, 16 * NT)

        @block.gpsimd
        def _(pool):
            pool.memset(ident[:, :], 0.0).then_inc(const_done, 1)
            pool.wait_ge(const_done, 1)
            pool.affine_select(out=ident[:, :], in_=ident[:, :], compare_op=ALU.not_equal, fill=1.0, base=0,
                               pattern=[[-1, P]], channel_multiplier=1).then_inc(const_done, 1)
            pool.wait_ge(dft_mm, 3 * 2 * HF)
            pool.iota(dist, pattern=[[-1, DIST_W]], base=S_SAMPLE - P, channel_multiplier=1,
                      allow_small_or_imprecise_dtypes=True).then_inc(iota_done, 1)
            pool.wait_ge(o_norm, NT)
            pool.wait_ge(ot_ev, NT)
            pool.iota(iota16, pattern=[[1, TOPK]], base=0, channel_multiplier=0,
                      allow_small_or_imprecise_dtypes=True).then_inc(iota_done, 1)
            pool.iota(iota_row, pattern=[[1, P]], base=0, channel_multiplier=0,
                      allow_small_or_imprecise_dtypes=True).then_inc(iota_done, 1)
            pool.wait_ge(iota_done, 3)
            with pool.Fori(0, ND) as i:
                pool.wait_ge(turn_ev, i + 1)
                for b in range(NB):
                    pool.wait_ge(g_mm, i * NB + b + 1)
                    pool.sem_inc(slots_free, 1)
                    for k in range(HOT_G):
                        t = GB_T * b + k
                        last = pool.tensor_scalar(hot[:, 0, 4 * (b % 2) + k, :], iota_row, slot_t[:, 0, t:t + 1],
                                                  slot_t[:, 2, t:t + 1], ALU.is_equal, ALU.mult)
                    last.then_inc(hot_g, 1)

            def lo_part(which, c, e):
                hi, lo, ready, done, used = ((uh_sb, ul_sb, uh_done, ul_done, h_mm),
                                             (vh_sb, vl_sb, vh_done, vl_done, y_mm))[which]
                pool.wait_ge(ready, c + 1)
                cols = slice(e * D, (e + 1) * D)
                pool.tensor_tensor(lo[:, cols], raw[:, e, :], hi[:, cols].bitcast(F32), ALU.subtract)\
                    .then_inc(done, 1)

            def tile(g, first, last):
                def copy_indices(dst, of, n):
                    pool.tensor_copy(dst, idx[:, bass.ds(of, 1), :].rearrange("p a s -> p (a s)"))\
                        .then_inc(idx_copied, 1)
                    pool.wait_ge(idx_copied, n)
                    pool.sem_inc(slots_free, 1)

                if first:
                    copy_indices(idx_u, 0, 1)
                for k in range(KP):
                    q = g * KP + k
                    s = [k * SP_]

                    def gather(n):
                        for _ in range(n):
                            v, slot = divmod(s[0], NSLOT)
                            pool.wait_ge(row_used[s[0] % RING], use(g, slot, v))
                            pool.sem_inc(slots_free, 1)
                            pool.indirect_dma_start(
                                ring[s[0] % RING], None, (pu, pv)[v],
                                bass.IndirectOffsetOnAxis(ap=(idx_u, idx_v)[v][:, slot:slot + 1], axis=0))\
                                .then_inc(row_in[s[0] % RING], 16)
                            s[0] += 1

                    if k == KP // 2 - 1:
                        copy_indices(idx_v, g, g * 2 + 2)
                    if k == KP - 1 and not last:
                        pool.wait_ge(acts, g + 1)
                        copy_indices(idx_u, g + 1, g * 2 + 3)
                    for what in POOL_ORDER.split():
                        if what[0] == "u":
                            if not (last and k == KP - 1):
                                lo_part(0, q * 2 + 2 + int(what[1]), int(what[1]))
                        elif what[0] == "v":
                            if not (first and k == 0):
                                lo_part(1, q * 2 + (int(what[1]) - 2), int(what[1]))
                        else:
                            gather(int(what))
                    assert s[0] == (k + 1) * SP_

            pool.wait_ge(started, 1)
            for k in range(RING):
                pool.sem_inc(row_used[k], 1)
            pool.sem_inc(ul_done, 1)
            pool.sem_inc(vl_done, 2)
            for e in range(2):
                lo_part(0, e, e)
            for m in range(2):
                pool.wait_ge(g_out[m], 16 * (ND + 1))
            tile(0, True, False)
            with pool.Fori(1, NG - 1) as g:
                tile(g, False, False)
            tile(NG - 1, False, True)
            for e in range(2):
                lo_part(1, 2 * NP - 2 + e, e)

        def att_groups(u, k):
            per_head = sum(nt * ((nt + 3) // 4) for _, nt in BATCHES)
            h, r = divmod(u, NT)
            n = h * per_head
            for _, nt in BATCHES:
                g = (nt + 3) // 4
                if r < nt:
                    return n + r * g + k // 4
                n += nt * g
                r -= nt

        @block.scalar
        def _(act_e):
            def evac(dst, src, func=ACT.Copy, **kw):
                return nc.scalar.activation(dst, src, func, **kw)

            act_e.wait_ge(var_done, 1)
            nc.scalar.activation(std, veps, ACT.Sqrt).then_inc(std_done, 1)
            for n in range(2 * NT):
                t, half = divmod(n, 2)
                act_e.wait_ge(xt_mm, n + 1)
                evac(xt[:, 4 * half:4 * half + 4, t * P:(t + 1) * P],
                     bank(n % 8).rearrange("p (c t) -> p c t", c=4)).then_inc(xt_ev, 1)
            n = 0
            for m in range(8):
                for a, b in token_blocks():
                    act_e.wait_ge(qk_mm, n + 1)
                    evac(qkv[:, m, a:b], bank(n % 8)[:, 0:b - a], scale=DQK ** -0.5 if m < 4 else 1.0)\
                        .then_inc(qk_ev, 1)
                    n += 1
            n = 0
            for m in range(2):
                for t in range(NT):
                    act_e.wait_ge(vf_mm, n + 1)
                    evac(vf[:, t, 512 * m:512 * m + 512], bank(n % 8)).then_inc(vf_ev, 1)
                    n += 1
            act_e.wait_ge(lam_dots, 1)
            nc.scalar.activation(elam, lam2, ACT.Exp).then_inc(lam_exp, 1)
            act_e.wait_ge(four_in, 64)
            for n in range(3):
                w = 512 if n < 2 else S_PROMPT
                tok = S_PROMPT + 512 * n if n < 2 else 0
                for j in range(2 * HF):
                    act_e.wait_ge(dft_mm, 2 * HF * n + j + 1)
                    if n > 0:
                        act_e.wait_ge(z_mm, HF * n)
                    evac(trig[:, j // HF, j % HF, 0:w], bank(j % 4)[:, 0:w]).then_inc(dft_ev, 1)
                for g in range(HF):
                    m = HF * n + g
                    act_e.wait_ge(z_mm, m + 1)
                    if m >= 2:
                        act_e.wait_ge(f_mm, m - 1)
                    evac(zt[:, m % 2, 0:w], bank(4 + m % 2)[:, 0:w]).then_inc(z_ev, 1)
                    act_e.wait_ge(f_mm, m + 1)
                    nc.scalar.activation(xt[:, 4 + g, tok:tok + w], bank(6 + m % 2)[:, 0:w], ACT.Identity,
                                         bias=bf[:, g:g + 1]).then_inc(f_ev, 1)
            u = 0
            for h in range(H):
                for t0, nt in BATCHES:
                    for qt in range(nt):
                        for c in range(2):
                            act_e.wait_ge(biased, 2 * u + c + 1)
                            keys = prob[:, c, 0:nt * P]
                            nc.scalar.activation(keys, keys, ACT.Exp, bias=nrmax[:, c:c + 1],
                                                 accum_out=psum_row[:, c:c + 1]).then_inc(exped, 1)
                        for k in range(0, nt, 4):
                            n = min(4, nt - k)
                            act_e.wait_ge(at_mm, att_groups(u, k) + 1)
                            if u:
                                act_e.wait_ge(pv_mm, u)
                            evac(difft[:, k:k + n, :], bank(k // 4)[:, 0:n * P].rearrange("p (k q) -> p k q", q=P))\
                                .then_inc(at_ev, 1)
                        u += 1
            act_e.wait_ge(ssq_done, 1)
            nc.scalar.activation(rms, ssq, ACT.Sqrt).then_inc(rms_done, 1)
            for t in range(NT):
                act_e.wait_ge(ot_mm, t + 1)
                evac(xt[:, 0:4, t * P:(t + 1) * P], bank(t % 8).rearrange("p (c t) -> p c t", c=4))\
                    .then_inc(ot_ev, 1)
            act_e.wait_ge(var_done, 2)
            nc.scalar.activation(std, veps, ACT.Sqrt).then_inc(std_done, 1)
            act_e.wait_ge(wo_mm, 2 * NT)
            for n in range(2 * NT):
                t, half = divmod(n, 2)
                act_e.wait_ge(x1t_mm, n + 1)
                evac(xt[:, 4 * half:4 * half + 4, t * P:(t + 1) * P],
                     bank(n % 8).rearrange("p (c t) -> p c t", c=4)).then_inc(x1t_ev, 1)
            n = 0
            for m in range(8):
                for a, b in token_blocks():
                    act_e.wait_ge(wq_mm, n + 1)
                    evac(qkv[:, m, a:b], bank(n % 8)[:, 0:b - a]).then_inc(wq_ev, 1)
                    n += 1
            for n in range(4 * NT):
                act_e.wait_ge(sc_mm, n + 1)
                evac(sc[:, n // 4, 512 * (n % 4):512 * (n % 4) + 512], bank(n % 8)).then_inc(sc_ev, 1)

            def load_scores(t):
                evac(scur.rearrange("p r n -> p (r n)"), sc[:, bass.ds(t, 1), :].rearrange("p a r -> p (a r)"))\
                    .then_inc(sc_cur, 1)

            def gate_exps(t):
                act_e.wait_ge(best_sub, t + 1)
                flat = best.rearrange("p h k -> p (h k)")
                nc.scalar.activation(flat, flat, ACT.Exp).then_inc(gate_exp, 1)

            act_e.wait_ge(sc_ev, 4 * NT)
            load_scores(0)
            with act_e.Fori(0, NG) as t:
                gate_exps(t)
                act_e.wait_ge(sc_used, t + 1)
                load_scores(t + 1)
            gate_exps(NG)
            act_e.wait_ge(sc_used, NG + 1)
            load_scores(NG + 1)

            def hot_j_rows(i, b):
                act_e.wait_ge(g_mm, i * NB + b + 1)
                for k in range(GB_T):
                    t = GB_T * b + k
                    last = nc.scalar.activation(hot[:, 1, 4 * (b % 2) + k, :], iota_row, ACT.Abs,
                                                bias=slot_t[:, 1, t:t + 1], scale=-1.0)
                last.then_inc(hot_dist, 1)

            def finish_hot_j(i, b):
                act_e.wait_ge(hot_dist, i * NB + b + 1)
                rows = hot[:, 1, 4 * (b % 2):4 * (b % 2) + GB_T, :]
                nc.scalar.activation(rows, rows, ACT.Relu, bias=iota_row[:, 1:2], scale=-1.0).then_inc(hot_j, 1)

            def store_bank(i, b):
                if b % (NB // 2) == 0:
                    act_e.wait_ge(g_out[b // (NB // 2)], i * 16 + 16)
                act_e.wait_ge(g_mm, i * NB + b + 3)
                t0 = GB_T * (b % (NB // 2))
                evac(spread[b // (NB // 2)][:, :, t0:t0 + GB_T],
                     bank(4 + b % 4).rearrange("p (t j) -> p j t", t=GB_T)).then_inc(g_ev, 1)

            def spread_tile(i, left):
                act_e.wait_ge(turn_mm, i + 1)
                act_e.wait_ge(g_mm, i * NB + 2)
                evac(slot_t, bank(0)[:, 0:3 * P].rearrange("p (w t) -> p w t", w=3)).then_inc(turn_ev, 1)
                act_e.wait_ge(turn_ev, i + 1)
                for b in range(NB + 2):
                    if left > 1 and b == LOAD_AT:
                        act_e.wait_ge(sc_used, i + (NG + 2))
                        load_scores(i + (NG + 2))
                    if left > 0 and b == EXP_AT:
                        gate_exps(i + (NG + 1))
                    if b < NB:
                        hot_j_rows(i, b)
                    if b >= 2:
                        store_bank(i, b - 2)
                    if b < NB:
                        finish_hot_j(i, b)

            act_e.sem_inc(g_ev, 4)
            act_e.sem_inc(hid_done, 2)
            with act_e.Fori(0, ND - 2) as i:
                spread_tile(i, 2)
            spread_tile(ND - 2, 1)
            spread_tile(ND - 1, 0)

            for n in range(2 * ND):
                t, half = divmod(n, 2)
                act_e.wait_ge(xh_mm, n + 1)
                evac(xh[:, 4 * half:4 * half + 4, t * P:(t + 1) * P],
                     bank(n % 8).rearrange("p (c t) -> p c t", c=4)).then_inc(xh_ev, 1)

            def hi_part(which, q, e):
                c = q * 2 + e
                if which == 0:
                    act_e.wait_ge(h_mm, c + 1)
                    act_e.wait_ge(u_in[e], q * 16 + 16)
                    evac(uh_sb[:, e * D:(e + 1) * D], raw[:, e, :]).then_inc(uh_done, 1)
                else:
                    act_e.wait_ge(y_mm, q * ND + 2 * ND)
                    act_e.wait_ge(v_in[e], q * 16 + 16)
                    evac(vh_sb[:, e * D:(e + 1) * D], raw[:, e, :]).then_inc(vh_done, 1)

            def load_x(g):
                evac(xcur, xn[:, bass.ds(g, 1), :].rearrange("p a n -> p (a n)")).then_inc(x_cur, 1)

            def peer_tile(g, last):
                for k in range(KP):
                    q = g * KP + k
                    def gelu(e):
                        c = q * 2 + e
                        act_e.wait_ge(h_mm, c + 3)
                        act_e.wait_ge(al_done, c + 2)
                        evac(hid.rearrange("p (h t) -> p h t", h=2),
                             act_psum[e][:, :, 0:HN], ACT.Gelu_apprx_tanh).then_inc(hid_done, 1)

                    def gated_hi(e):
                        act_e.wait_ge(gated, q * 2 + e + 2)
                        if e == 0:
                            act_e.wait_ge(y_mm, q * ND + ND)
                        evac(ah[:, k % 2, e, :], hid).then_inc(ah_done, 1)

                    gelu(0)
                    if not (last and k == KP - 1):
                        for e in range(2):
                            hi_part(0, q + 1, e)
                    gated_hi(0)
                    gelu(1)
                    gated_hi(1)
                    if k == KP - 1 and not last:
                        act_e.wait_ge(coefs, g * 2 + 2)
                        load_x(g + 1)
                    for e in range(2):
                        hi_part(1, q, e)
                    if k == KP // 2 - 1:
                        act_e.wait_ge(acts, g + 1)
                        evac(gact, act, ACT.Gelu_apprx_tanh).then_inc(gacts, 1)

            act_e.wait_ge(started, 1)
            for e in range(2):
                act_e.wait_ge(u_in[e], 16)
                evac(uh_sb[:, e * D:(e + 1) * D], raw[:, e, :]).then_inc(uh_done, 1)
            act_e.wait_ge(g_out[1], 16 * (ND + 1))
            load_x(0)
            with act_e.Fori(0, NG - 1) as g:
                peer_tile(g, False)
            peer_tile(NG - 1, True)
            act_e.wait_ge(var_done, 3)
            nc.scalar.activation(std, veps, ACT.Sqrt).then_inc(std_done, 1)

        @block.tensor
        def _(pe):
            pe.wait_ge(const_done, 2)
            for n in range(2 * NT):
                t, half = divmod(n, 2)
                if half == 0:
                    pe.wait_ge(ln_in_done, t + 1)
                if n >= 8:
                    pe.wait_ge(xt_ev, n - 7)
                for c in range(4):
                    j = 4 * half + c
                    last = nc.tensor.transpose(bank(n % 8)[:, c * P:(c + 1) * P], xn[:, t, j * P:(j + 1) * P],
                                               ident[:, :])
                last.then_inc(xt_mm, 1)
            pe.wait_ge(xt_ev, 2 * NT)
            n = 0
            for m in range(8):
                pe.wait_ge(w_qk_in[m], 16)
                for a, b in token_blocks():
                    if n >= 8:
                        pe.wait_ge(qk_ev, n - 7)
                    for c in range(DC):
                        last = nc.tensor.matmul(bank(n % 8)[:, 0:b - a], w8[:, m, c, :], xt[:, c, a:b],
                                                start=(c == 0), stop=(c == DC - 1))
                    last.then_inc(qk_mm, 1)
                    n += 1
            pe.wait_ge(qk_ev, 8 * len(token_blocks()))
            n = 0
            for m in range(2):
                pe.wait_ge(w_vf_in[m], 16)
                for t in range(NT):
                    if n >= 8:
                        pe.wait_ge(vf_ev, n - 7)
                    for c in range(DC):
                        last = nc.tensor.matmul(bank(n % 8), xt[:, c, t * P:(t + 1) * P], w2[:, m, c, :],
                                                start=(c == 0), stop=(c == DC - 1))
                    last.then_inc(vf_mm, 1)
                    n += 1
            pe.wait_ge(vf_ev, 2 * NT)
            pe.wait_ge(four_in, 64)
            for n in range(3):
                w, t0, nc_k = (512, 2, 8) if n < 2 else (S_PROMPT, 0, 2)
                for j in range(2 * HF):
                    k, g = divmod(j, HF)
                    if g == 0:
                        pe.wait_ge(dft_in[k], 16 * (n + 1))
                    if 2 * HF * n + j >= 4:
                        pe.wait_ge(dft_ev, 2 * HF * n + j - 3)
                    for c in range(nc_k):
                        last = nc.tensor.matmul(bank(j % 4)[:, 0:w], vf[:, t0 + c, 512 + g * P:512 + (g + 1) * P],
                                                w2[:, k, c, 0:w], start=(c == 0), stop=(c == nc_k - 1))
                    last.then_inc(dft_mm, 1)
                for g in range(HF):
                    m = HF * n + g
                    pe.wait_ge(dft_ev, 2 * HF * n + HF + g + 1)
                    if m >= 2:
                        pe.wait_ge(z_ev, m - 1)
                    nc.tensor.matmul(bank(4 + m % 2)[:, 0:w], cc, trig[:, 0, g, 0:w], start=True, stop=False)
                    nc.tensor.matmul(bank(4 + m % 2)[:, 0:w], scn, trig[:, 1, g, 0:w], start=False, stop=True)\
                        .then_inc(z_mm, 1)
                    pe.wait_ge(z_ev, m + 1)
                    if m >= 2:
                        pe.wait_ge(f_ev, m - 1)
                    nc.tensor.matmul(bank(6 + m % 2)[:, 0:w], wf[:, g, :], zt[:, m % 2, 0:w],
                                     start=True, stop=True).then_inc(f_mm, 1)
            pe.wait_ge(f_ev, 3 * HF)

            units = [(h, t0, nt, qt) for h in range(H) for t0, nt in BATCHES for qt in range(nt)]

            def scores(u):
                h, t0, nt, qt = units[u]
                q0, k0 = (t0 + qt) * P, t0 * P
                for c in range(2):
                    if u:
                        pe.wait_ge(biased, 2 * (u - 1) + c + 1)
                    rows = slice(c * DQK, (c + 1) * DQK)
                    for k in range(0, nt * P, 512):
                        w = min(512, nt * P - k)
                        last = nc.tensor.matmul(wide[c][:, k:k + w], qkv[rows, h, q0:q0 + P],
                                                qkv[rows, 4 + h, k0 + k:k0 + k + w], start=True, stop=True)
                    last.then_inc(s_mm, 1)

            def mix_values(u):
                h, t0, nt, qt = units[u]
                pe.wait_ge(diffed, u + 1)
                for k in range(0, nt, 4):
                    if att_groups(u, k) >= 1:
                        pe.wait_ge(at_ev, max(1, att_groups(u, 0)))
                    for j in range(k, min(k + 4, nt)):
                        last = nc.tensor.transpose(bank(k // 4)[:, (j - k) * P:(j - k + 1) * P],
                                                   diff[:, j * P:(j + 1) * P], ident[:, :])
                    last.then_inc(at_mm, 1)
                for j in range(nt):
                    if j % 4 == 0:
                        pe.wait_ge(at_ev, att_groups(u, j) + 1)
                    if u >= 2 and j == 0:
                        pe.wait_ge(o_ev, u - 1)
                    last = nc.tensor.matmul(bank(2 + u % 2)[:, 0:P], difft[:, j, :], vf[:, t0 + j, h * P:(h + 1) * P],
                                            start=(j == 0), stop=(j == nt - 1))
                last.then_inc(pv_mm, 1)

            scores(0)
            for u in range(len(units)):
                if u + 1 < len(units):
                    scores(u + 1)
                mix_values(u)
            for t in range(NT):
                pe.wait_ge(o_norm, t + 1)
                if t >= 8:
                    pe.wait_ge(ot_ev, t - 7)
                for h in range(H):
                    last = nc.tensor.transpose(bank(t % 8)[:, h * P:(h + 1) * P],
                                               vf[:, t, 512 + h * P:512 + (h + 1) * P], ident[:, :])
                last.then_inc(ot_mm, 1)
            pe.wait_ge(w_out_in, 16)
            pe.wait_ge(ot_ev, NT)
            for n in range(2 * NT):
                t, half = divmod(n, 2)
                if n >= 8:
                    pe.wait_ge(wo_add, n - 7)
                for c in range(DC):
                    last = nc.tensor.matmul(bank(n % 8), xt[:, c, t * P:(t + 1) * P],
                                            wfull[:, c, 512 * half:512 * half + 512],
                                            start=(c == 0), stop=(c == DC - 1))
                last.then_inc(wo_mm, 1)
            pe.wait_ge(wo_add, 2 * NT)
            for n in range(2 * NT):
                t, half = divmod(n, 2)
                if half == 0:
                    pe.wait_ge(x1_done, t + 1)
                if n >= 8:
                    pe.wait_ge(x1t_ev, n - 7)
                for c in range(4):
                    j = 4 * half + c
                    last = nc.tensor.transpose(bank(n % 8)[:, c * P:(c + 1) * P], xn[:, t, j * P:(j + 1) * P],
                                               ident[:, :])
                last.then_inc(x1t_mm, 1)
            pe.wait_ge(x1t_ev, 2 * NT)
            n = 0
            for m in range(8):
                pe.wait_ge(wq_in[m], 16)
                for a, b in token_blocks():
                    if n >= 8:
                        pe.wait_ge(wq_ev, n - 7)
                    for c in range(DC):
                        last = nc.tensor.matmul(bank(n % 8)[:, 0:b - a], w8[:, m, c, :], xt[:, c, a:b],
                                                start=(c == 0), stop=(c == DC - 1))
                    last.then_inc(wq_mm, 1)
                    n += 1
            pe.wait_ge(wq_ev, 8 * len(token_blocks()))
            pe.wait_ge(sk_in, 16)
            for n in range(4 * NT):
                t, c, h4 = n // 4, (n % 4) // 2, n % 2
                if n >= 8:
                    pe.wait_ge(sc_ev, n - 7)
                rows = slice(c * DQK, (c + 1) * DQK)
                for j in range(4):
                    h = 4 * h4 + j
                    last = nc.tensor.matmul(bank(n % 8)[:, j * NK:(j + 1) * NK], qkv[rows, h, t * P:(t + 1) * P],
                                            sk[rows, h, :], start=True, stop=True)
                last.then_inc(sc_mm, 1)
            pe.wait_ge(sc_ev, 4 * NT)

            pe.sem_inc(g_mm, 2)
            pe.sem_inc(h_mm, 2)
            pe.sem_inc(y_mm, 2 * ND)
            with pe.Fori(0, ND) as i:
                pe.wait_ge(retrieved, i + (NG + 1))
                for w, m in enumerate((iab[:, 0, :], iab[:, 1, :], gate)):
                    last = nc.tensor.transpose(bank(0)[:, w * P:(w + 1) * P], m, ident[:, :])
                last.then_inc(turn_mm, 1)
                for b in range(NB):
                    pe.wait_ge(hot_g, i * NB + b + 1)
                    pe.wait_ge(hot_v, i * NB + b + 1)
                    pe.wait_ge(hot_j, i * NB + b + 1)
                    pe.wait_ge(g_ev, i * NB + b + 1)
                    for k in range(GB_T):
                        r = 4 * (b % 2) + k
                        last = nc.tensor.matmul(bank(4 + b % 4)[:, k * P:(k + 1) * P], hot[:, 0, r, :],
                                                hot[:, 1, r, :], start=True, stop=True)
                    last.then_inc(g_mm, 1)
            for n in range(2 * ND):
                t, half = divmod(n, 2)
                if n >= 8:
                    pe.wait_ge(xl_ev, n - 7)
                else:
                    pe.wait_ge(g_ev, ND * NB + 4)
                for c in range(4):
                    j = 4 * half + c
                    last = nc.tensor.transpose(bank(n % 8)[:, c * P:(c + 1) * P], xn[:, NG + t, j * P:(j + 1) * P],
                                               ident[:, :])
                last.then_inc(xh_mm, 1)
            pe.wait_ge(xl_ev, 2 * ND)

            def activations(q, e):
                c = q * 2 + e
                pe.wait_ge(uh_done, c + 1)
                pe.wait_ge(ul_done, c + 2)
                pe.wait_ge(hid_done, c + 1)
                for k in range(DC):
                    for lhs, rhs in ((uh, xh), (uh, xl), (ul, xh)):
                        for h in range(2):
                            last = nc.tensor.matmul(
                                act_psum[e][:, h, 0:HN], lhs[:, e, k, :], rhs[:, k, h * HN:(h + 1) * HN],
                                start=(k == 0 and rhs is xh and lhs is uh), stop=(k == DC - 1 and lhs is ul))
                last.then_inc(h_mm, 1)

            def sums(q, par):
                pe.wait_ge(ah_done, q * 2 + 2)
                pe.wait_ge(al_done, q * 2 + 4)
                pe.wait_ge(vh_done, q * 2 + 2)
                pe.wait_ge(vl_done, q * 2 + 4)
                for t in range(ND):
                    pe.wait_ge(y_add, q * ND + t + (ND - 1))
                    toks = slice(t * P, (t + 1) * P)
                    for e in range(2):
                        for n, (lhs, rhs) in enumerate(((ah, vh), (ah, vl), (al, vh))):
                            for h in range(2):
                                last = nc.tensor.matmul(
                                    wide[t % 2][:, 512 * h:512 * h + 512], lhs[:, par, e, toks],
                                    rhs[:, e, 512 * h:512 * h + 512], start=(e == 0 and n == 0),
                                    stop=(e == 1 and n == 2))
                    last.then_inc(y_mm, 1)

            for e in range(2):
                activations(0, e)
            with pe.Fori(0, NP // 2 - 1) as i:
                for par in range(2):
                    for e in range(2):
                        activations(i * 2 + (par + 1), e)
                    sums(i * 2 + par, par)
            for e in range(2):
                activations(NP - 1, e)
            sums(NP - 2, 0)
            sums(NP - 1, 1)

        @block.vector
        def _(dve):
            done = [0]

            def link(ins):
                done[0] += 1
                ins.then_inc(dve_chain, 1)
                dve.wait_ge(dve_chain, done[0])

            def ln_stats(t):
                for j in range(2):
                    link(nc.vector.bn_stats(stats[:, t, 6 * j:6 * j + 6], xn[:, t, 512 * j:512 * j + 512]))
                link(nc.vector.bn_aggr(mv[:, t, :], stats[:, t, :]))

            def ln_apply(which, ready):
                nc.vector.tensor_scalar(veps, mv[:, :, 1], EPS, None, ALU.add).then_inc(var_done, 1)
                dve.wait_ge(std_done, which + 1)
                link(nc.vector.reciprocal(rstd, std))
                dve.wait_ge(gain_in[which], 32)
                for t in range(NT):
                    r = xn[:, t, :]
                    link(nc.vector.scalar_tensor_tensor(out=r, in0=r, scalar=mv[:, t, 0:1], in1=g_row,
                                                        op0=ALU.subtract, op1=ALU.mult))
                    nc.vector.scalar_tensor_tensor(out=r, in0=r, scalar=rstd[:, t:t + 1], in1=b_row,
                                                   op0=ALU.mult, op1=ALU.add).then_inc(ready, 1)

            for t in range(NT):
                dve.wait_ge(x_in[t], 16)
                ln_stats(t)
            ln_apply(0, ln_in_done)
            dve.wait_ge(lam_in, 80)
            for a in range(2):
                link(nc.vector.tensor_tensor_reduce(lam4[:, 2 * a, :], lam4[:, 2 * a, :], lam4[:, 2 * a + 1, :],
                                                    1.0, 0.0, ALU.mult, ALU.add, lam2[:, a:a + 1]))
            nc.vector.tensor_scalar(lam2, lam2, 0.0, None, ALU.add).then_inc(lam_dots, 1)
            dve.wait_ge(lam_exp, 1)
            link(nc.vector.tensor_scalar(nlam, elam[:, 1:2], elam[:, 0:1], -LAMBDA_INIT, ALU.subtract, ALU.add))
            link(nc.vector.tensor_scalar(sub_g, sub_g, OUT_SCALE, None, ALU.mult))

            dve.wait_ge(iota_done, 1)
            link(nc.vector.tensor_scalar(bias_h, dist, -1.0, None, ALU.mult))
            link(nc.vector.tensor_tensor(dist, dist, bias_h, ALU.max))
            u = 0

            def take_output(v, h, tq):
                dve.wait_ge(pv_mm, v + 1)
                o = vf[:, tq, 512 + h * P:512 + (h + 1) * P]
                nc.vector.tensor_copy(o, bank(2 + v % 2)[:, 0:P]).then_inc(o_ev, 1)
                dve.wait_ge(o_ev, v + 1)
                n = tq * H + h
                link(nc.vector.tensor_tensor_reduce(scratch, o, o, 1.0 / P, EPS, ALU.mult, ALU.add, ssq[:, n:n + 1]))

            units = [(h, t0, nt, qt) for h in range(H) for t0, nt in BATCHES for qt in range(nt)]
            for u, (h, t0, nt, qt) in enumerate(units):
                if u % NT == 0:
                    link(nc.vector.tensor_scalar(bias_h, dist, -SLOPES[h], None, ALU.mult))
                w = nt * P
                first = S_SAMPLE - P - qt * P
                for c in range(2):
                    dve.wait_ge(s_mm, 2 * u + c + 1)
                    link(nc.vector.tensor_tensor_reduce(prob[:, c, 0:w], wide[c][:, 0:w], bias_h[:, first:first + w],
                                                        1.0, -3.0e38, ALU.add, ALU.max, rmax[:, c:c + 1]))
                    nc.vector.tensor_scalar(nrmax[:, c:c + 1], rmax[:, c:c + 1], -1.0, None, ALU.mult)\
                        .then_inc(biased, 1)
                if u >= 1:
                    hh, tt0, _, qq = units[u - 1]
                    take_output(u - 1, hh, tt0 + qq)
                dve.wait_ge(exped, 2 * u + 2)
                link(nc.vector.reciprocal(rinv, psum_row))
                link(nc.vector.tensor_scalar(rinv[:, 1:2], rinv[:, 1:2], nlam, None, ALU.mult))
                if u:
                    dve.wait_ge(at_mm, att_groups(u, 0))
                link(nc.vector.tensor_scalar(diff[:, 0:w], prob[:, 0, 0:w], rinv[:, 0:1], None, ALU.mult))
                nc.vector.scalar_tensor_tensor(out=diff[:, 0:w], in0=prob[:, 1, 0:w], scalar=rinv[:, 1:2],
                                               in1=diff[:, 0:w], op0=ALU.mult, op1=ALU.add).then_inc(diffed, 1)
                dve.wait_ge(diffed, u + 1)
            hh, tt0, _, qq = units[-1]
            take_output(len(units) - 1, hh, tt0 + qq)
            nc.vector.tensor_scalar(ssq, ssq, 0.0, None, ALU.add).then_inc(ssq_done, 1)
            dve.wait_ge(rms_done, 1)
            link(nc.vector.reciprocal(rrms, rms))
            for t in range(NT):
                for h in range(H):
                    o = vf[:, t, 512 + h * P:512 + (h + 1) * P]
                    last = nc.vector.scalar_tensor_tensor(out=o, in0=o, scalar=rrms[:, t * H + h:t * H + h + 1],
                                                          in1=sub_g, op0=ALU.mult, op1=ALU.mult)
                last.then_inc(o_norm, 1)
            for n in range(2 * NT):
                t, half = divmod(n, 2)
                dve.wait_ge(wo_mm, n + 1)
                r = xn[:, t, 512 * half:512 * half + 512]
                nc.vector.scalar_tensor_tensor(out=r, in0=r, scalar=ALPHA, in1=bank(n % 8),
                                               op0=ALU.mult, op1=ALU.add).then_inc(wo_add, 1)
                dve.wait_ge(wo_add, n + 1)
                if half:
                    ln_stats(t)
            ln_apply(1, x1_done)

            steps = [0]

            def step(ins):
                steps[0] += 1
                ins.then_inc(chain, 1)
                dve.wait_ge(chain, steps[0])

            def behind(ins):
                steps[0] += 1
                ins.then_inc(chain, 1)
                if steps[0] > 1:
                    dve.wait_ge(chain, steps[0] - 1)

            def restart():
                dve.wait_ge(chain, steps[0])
                dve.sem_clear(chain)
                steps[0] = 0

            def retrieval(t, gathers):
                def begin():
                    dve.wait_ge(sc_cur, t + 1)
                    dve.sem_inc(scores_seen, 1)

                def top8(k, two):
                    if steps[0]:
                        dve.wait_ge(chain, steps[0])
                    for v, _, row in two:
                        behind(nc.vector.max(v[:, 8 * k:8 * k + 8], row))
                    for v, i, row in two:
                        behind(nc.vector.max_index(i[:, 8 * k:8 * k + 8], v[:, 8 * k:8 * k + 8], row))
                    if k == 0:
                        for v, _, row in two:
                            behind(nc.vector.match_replace(row, v[:, 0:8], row, NEG))

                def rows(r, k):
                    if r == 0 and k == 0:
                        begin()
                    top8(k, [(vals[:, n, :], iu[:, n, :], scur[:, n, :]) for n in (r, r + 1)])

                def sums():
                    dve.wait_ge(chain, steps[0])
                    nc.vector.tensor_copy(idf, iu.rearrange("p r k -> p (r k)")).then_inc(sc_used, 1)
                    dve.wait_ge(sc_used, t + 1)
                    c4 = cand.rearrange("p (h a b) -> p h a b", h=PH, a=TOPK)
                    shape = [P, PH, TOPK, TOPK]
                    step(nc.vector.tensor_tensor(c4, vals[:, 0:PH, :].unsqueeze(3).broadcast_to(shape),
                                                 vals[:, PH:2 * PH, :].unsqueeze(2).broadcast_to(shape), ALU.add))

                def heads(h, k):
                    c = cand.rearrange("p (h n) -> p h n", h=PH)
                    top8(k, [(best[:, n, :], posu[:, n, :], c[:, n, :]) for n in (h, h + 1)])

                def positions():
                    dve.wait_ge(chain, steps[0])
                    flat = posu.rearrange("p h k -> p (h k)")
                    step(nc.vector.tensor_scalar(pshift, flat, 4, None, ALU.logical_shift_right))
                    step(nc.vector.tensor_copy(pabf[:, 0, :], pshift))
                    step(nc.vector.tensor_scalar(pshift, flat, TOPK - 1, None, ALU.bitwise_and))
                    step(nc.vector.tensor_copy(pabf[:, 1, :], pshift))

                def lookup(c, part):
                    p3 = pick.rearrange("p (s a) -> p s a", a=TOPK)
                    if part == 0:
                        step(nc.vector.tensor_tensor(
                            p3, pabf[:, c, :].unsqueeze(2).broadcast_to([P, NSLOT, TOPK]),
                            iota16.unsqueeze(1).broadcast_to([P, NSLOT, TOPK]), ALU.is_equal))
                    elif part == 1:
                        shape = [P, PH, TOPK, TOPK]
                        p4 = pick.rearrange("p (h k a) -> p h k a", h=PH, k=TOPK)
                        rows = idf.rearrange("p (r k) -> p r k", r=2 * PH)[:, c * PH:(c + 1) * PH, :]
                        step(nc.vector.tensor_tensor(p4, p4, rows.unsqueeze(2).broadcast_to(shape), ALU.mult))
                    else:
                        step(nc.vector.tensor_reduce(iab[:, c, :], p3, AX.X, ALU.add))

                def indices():
                    if gathers:
                        step(nc.vector.scalar_tensor_tensor(out=eidf, in0=iab[:, 0, :], scalar=float(NK),
                                                            in1=iab[:, 1, :], op0=ALU.mult, op1=ALU.add))
                        step(nc.vector.tensor_copy(idx[:, bass.ds(t, 1), :].rearrange("p a s -> p (a s)"), eidf))

                def gates_a():
                    step(nc.vector.tensor_copy(mx8, best[:, :, 0]))
                    nc.vector.tensor_tensor(best, best, mx8.unsqueeze(2).broadcast_to([P, PH, TOPK]),
                                            ALU.subtract).then_inc(best_sub, 1)

                def gates_b():
                    dve.wait_ge(gate_exp, t + 1)
                    step(nc.vector.tensor_reduce(gsum, best, AX.X, ALU.add))
                    step(nc.vector.reciprocal(gsum, gsum))
                    dst = gates_g[:, bass.ds(t, 1), :].rearrange("p a s -> p (a s)") if gathers else gate
                    nc.vector.tensor_tensor(dst.rearrange("p (h k) -> p h k", h=PH), best,
                                            gsum.unsqueeze(2).broadcast_to([P, PH, TOPK]), ALU.mult)\
                        .then_inc(retrieved, 1)

                out_p = [lambda r=r, k=k: rows(r, k) for r in range(0, 2 * PH, 2) for k in range(2)] + [sums]
                out_p += [lambda h=h, k=k: heads(h, k) for h in range(0, PH, 2) for k in range(2)] + [gates_a, positions]
                out_p += [lambda c=c, k=k: lookup(c, k) for c in range(2) for k in range(3)]
                return out_p + [indices, gates_b]

            dve.wait_ge(iota_done, 3)
            with dve.Fori(0, NG) as t:
                for piece in retrieval(t, True):
                    piece()
                restart()
            for piece in retrieval(NG, False):
                piece()
            restart()

            def hot_rows(i, b):
                dve.wait_ge(g_mm, i * NB + b + 1)
                for k in range(HOT_G, GB_T):
                    t = GB_T * b + k
                    last = nc.vector.tensor_scalar(hot[:, 0, 4 * (b % 2) + k, :], iota_row, slot_t[:, 0, t:t + 1],
                                                   slot_t[:, 2, t:t + 1], ALU.is_equal, ALU.mult)
                last.then_inc(hot_v, 1)

            with dve.Fori(0, ND - 1) as i:
                dve.wait_ge(turn_ev, i + 1)
                pieces = retrieval(i + (NG + 1), False)
                for b in range(NB):
                    for piece in pieces[(b * len(pieces) + NB - 1) // NB:((b + 1) * len(pieces) + NB - 1) // NB]:
                        piece()
                    hot_rows(i, b)
                restart()
            dve.wait_ge(turn_ev, ND)
            for b in range(NB):
                hot_rows(ND - 1, b)

            for n in range(2 * ND):
                t, half = divmod(n, 2)
                cols = slice(t * P, (t + 1) * P)
                rows = slice(4 * half, 4 * half + 4)
                dve.wait_ge(xh_ev, n + 1)
                nc.vector.tensor_tensor(xl[:, rows, cols], bank(n % 8).rearrange("p (c t) -> p c t", c=4),
                                        xh[:, rows, cols].bitcast(F32), ALU.subtract).then_inc(xl_ev, 1)
            dve.wait_ge(xl_ev, 2 * ND)
            dve.sem_inc(started, 1)
            for t in range(ND):
                nc.vector.tensor_scalar(xn[:, NG + t, :], xn[:, NG + t, :], ALPHA, None, ALU.mult)\
                    .then_inc(y_add, 1)
            dve.sem_inc(gated, 1)
            dve.sem_inc(al_done, 2)

            def tile(g, first, last):
                y = xn[:, bass.ds(g, 1), :].rearrange("p a n -> p (a n)")

                def slot(s):
                    k, (v, c) = s % RING, divmod(s, NSLOT)
                    dve.wait_ge(row_in[k], use(g, c, v) * 16)
                    if v == 0:
                        nc.vector.tensor_tensor_reduce(ring[k], ring[k], xcur, 1.0, 0.0, ALU.mult, ALU.add,
                                                       act[:, c:c + 1]).then_inc(row_used[k], 1)
                    else:
                        if c:
                            dve.wait_ge(row_used[(c - 1) % RING], use(g, c - 1, 1) + 1)
                        nc.vector.scalar_tensor_tensor(out=y, in0=ring[k], scalar=coef[:, c:c + 1], in1=y,
                                                       op0=ALU.mult, op1=ALU.add).then_inc(row_used[k], 1)

                def coefficients():
                    for k in range(RING):
                        dve.wait_ge(row_used[k], use(g, NSLOT - RING + k, 0) + 1)
                    dve.sem_inc(acts, 1)
                    dve.wait_ge(gacts, g + 1)
                    nc.vector.tensor_tensor(coef, gact, gates_g[:, bass.ds(g, 1), :].rearrange("p a s -> p (a s)"),
                                            ALU.mult).then_inc(coefs, 1)
                    nc.vector.tensor_scalar(y, xcur, ALPHA, None, ALU.mult).then_inc(coefs, 1)
                    dve.wait_ge(coefs, g * 2 + 2)

                def gated_part(q, e):
                    dve.wait_ge(hid_done, q * 2 + e + 3)
                    dve.wait_ge(g_in, q * 32 + 16 * (e + 1))
                    nc.vector.tensor_tensor(hid, hid, g_in_sb, ALU.mult).then_inc(gated, 1)

                def lo_part(q, par, e):
                    dve.wait_ge(ah_done, q * 2 + e + 1)
                    nc.vector.tensor_tensor(al[:, par, e, :], hid, ah[:, par, e, :].bitcast(F32),
                                            ALU.subtract).then_inc(al_done, 1)

                dve.wait_ge(x_cur, g + 1)
                for k in range(KP):
                    q, par = g * KP + k, k % 2
                    s = [k * SP_]

                    if k == KP // 2:
                        coefficients()
                    t = 0
                    for what in DVE_ORDER.split():
                        if what[0] == "g":
                            gated_part(q, int(what[1]))
                        elif what[0] == "l":
                            lo_part(q, par, int(what[1]))
                        elif what == "a":
                            if not (first and k == 0):
                                add(q, t)
                            t += 1
                        else:
                            for _ in range(int(what)):
                                slot(s[0])
                                s[0] += 1
                    assert s[0] == (k + 1) * SP_ and t == ND

            def add(q, t):
                n = q * ND + (t - ND)
                dve.wait_ge(y_mm, n + (2 * ND + 1))
                dve.wait_ge(y_add, n + 1)
                nc.vector.tensor_tensor(xn[:, NG + t, :], xn[:, NG + t, :], wide[t % 2][:, :], ALU.add)\
                    .then_inc(y_add, 1)

            tile(0, True, False)
            with dve.Fori(1, NG - 1) as g:
                tile(g, False, False)
            tile(NG - 1, False, True)
            for k in range(RING):
                dve.wait_ge(row_used[k], use(NG - 1, NSLOT - RING + k, 1) + 1)
            for t in range(NG):
                ln_stats(t)
            for t in range(ND):
                add(NP, t)
                dve.wait_ge(y_add, ND * NP + t + 1)
                ln_stats(NG + t)
            ln_apply(2, y_done)


def dft_tables(n, scale):
    a = 2.0 * np.pi * ((np.arange(n)[:, None] * np.arange(n)[None, :]) % n) / n
    return np.cos(a) * scale, np.sin(a) * scale


def kernel(**inputs):
    import numpy as _np
    import concourse.bacc as _bacc
    from concourse.bass_utils import run_bass_kernel_spmd as _run

    f = {k: _np.asarray(v) for k, v in inputs.items()}
    c, s = dft_tables(P, 1.0)
    arrays = {
        "x": _np.concatenate([f["x_prompt"][0], f["x_sample"][0]], axis=0),
        "ln_g": f["ln_in_g"], "ln_b": f["ln_in_b"], "w_in": f["w_in"][0],
        "lq1": f["lambda_q1"][0], "lk1": f["lambda_k1"][0], "lq2": f["lambda_q2"][0], "lk2": f["lambda_k2"][0],
        "subln_g": f["subln_g"][0], "w_f": f["w_fourier"][0], "b_f": f["b_fourier"][0], "w_out": f["w_out"][0],
        "ln1_g": f["ln1_g"][0], "ln1_b": f["ln1_b"][0], "wq": f["peer_wq"][0],
        "skt": _np.ascontiguousarray(f["peer_subkeys"][0].transpose(1, 3, 0, 2)).reshape(2, DQK, PH, NK),
        "pu": f["peer_u"][0],
        "ut": f["peer_u"][0].reshape(P, NK, DC, P).transpose(1, 3, 2, 0).reshape(NK, P, D),
        "pv": f["peer_v"][0], "ln2_g": f["ln2_g"][0], "ln2_b": f["ln2_b"][0],
        "dft_sample": _np.stack(dft_tables(S_SAMPLE, (S_SAMPLE * P) ** -0.5)).astype(_np.float32),
        "dft_prompt": _np.stack(dft_tables(S_PROMPT, (S_PROMPT * P) ** -0.5)).astype(_np.float32),
        "dft_chan": _np.stack([c, -s]).astype(_np.float32),
    }
    nc = _bacc.Bacc("TRN2", target_bir_lowering=False, num_devices=1)
    args, feed = [], {}
    for name, a in arrays.items():
        feed[f"in_{name}"] = _np.ascontiguousarray(a)
        args.append(nc.dram_tensor(f"in_{name}", a.shape, F32, kind="ExternalInput").ap())
    args.append(nc.dram_tensor("spread_gates", (NK, P, TD), F32, kind="Internal").ap())
    args.append(nc.dram_tensor("out_y", (T, D), F32, kind="ExternalOutput").ap())
    build(nc, *args)
    r = _run(nc, [feed], core_ids=[0])
    y = r.results[0]["out_y"]
    return y[None, :S_PROMPT], y[None, S_PROMPT:]
```
